# Optimizing a Trainium2 kernel written in Bass

```python
import jax, jax.numpy as jnp
from jax import lax
import numpy as np

D_MODEL = 1024
BATCH = 1
SEQ = 512
DEPTH = 1

EPS = 1e-6
ROPE_THETA = 10000.0
NEG_INF = -1e30

SWA_HEADS = 8
SWA_KV_HEADS = 2
SWA_GROUP = SWA_HEADS // SWA_KV_HEADS
SWA_HEAD_DIM = 64
SWA_WINDOW = 128
SWA_BLOCK = 128

MLA_HEADS = 8
MLA_Q_RANK = 256
MLA_KV_RANK = 128
MLA_NOPE_DIM = 64
MLA_ROPE_DIM = 32
MLA_V_DIM = 64
MLA_QK_DIM = MLA_NOPE_DIM + MLA_ROPE_DIM
MLA_Q_BLOCK = 128

SWA_WIDTH = SWA_HEADS * SWA_HEAD_DIM
MLA_WIDTH = MLA_HEADS * MLA_V_DIM
MIX_WIDTH = SWA_WIDTH + MLA_WIDTH

IN_SIZES = (SWA_HEADS * SWA_HEAD_DIM,
            SWA_KV_HEADS * SWA_HEAD_DIM,
            SWA_KV_HEADS * SWA_HEAD_DIM,
            MLA_Q_RANK,
            MLA_KV_RANK,
            MLA_ROPE_DIM)
IN_WIDTH = int(sum(IN_SIZES))
IN_SPLITS = tuple(int(v) for v in np.cumsum(IN_SIZES)[:-1])

PEER_HEADS = 8
PEER_N_KEYS = 128
PEER_EXPERTS = PEER_N_KEYS * PEER_N_KEYS
PEER_QUERY_DIM = 256
PEER_HALF_DIM = PEER_QUERY_DIM // 2
PEER_TOPK = 16
PEER_TOKEN_BLOCK = 128

N_MOD = 6


def rmsnorm(x, gain=None):
    xf = x.astype(jnp.float32)
    y = xf * lax.rsqrt(jnp.mean(xf * xf, axis=-1, keepdims=True) + EPS)
    if gain is not None:
        y = y * gain.astype(jnp.float32)
    return y.astype(x.dtype)

def modulate(h, shift, scale):
    return h * (1.0 + scale[:, None, :]) + shift[:, None, :]

def rope_tables(seq, dim):
    inv = 1.0 / (ROPE_THETA ** (jnp.arange(0, dim, 2, dtype=jnp.float32) / dim))
    ang = jnp.arange(seq, dtype=jnp.float32)[:, None] * inv[None, :]
    return jnp.cos(ang), jnp.sin(ang)

def apply_rope(x, cos, sin):
    xf = x.astype(jnp.float32)
    half = xf.shape[-1] // 2
    x1, x2 = xf[..., :half], xf[..., half:]
    c = cos[None, :, None, :]
    s = sin[None, :, None, :]
    return jnp.concatenate([x1 * c - x2 * s, x2 * c + x1 * s], axis=-1).astype(x.dtype)

def windowed_gqa(q, k, v, sink):
    B, S = q.shape[0], q.shape[1]
    nb = S // SWA_BLOCK
    cos, sin = rope_tables(S, SWA_HEAD_DIM)
    q = apply_rope(q, cos, sin)
    k = apply_rope(k, cos, sin)
    qb = q.reshape(B, nb, SWA_BLOCK, SWA_KV_HEADS, SWA_GROUP, SWA_HEAD_DIM)
    pad = ((0, 0), (SWA_BLOCK, SWA_BLOCK), (0, 0), (0, 0))
    kp = jnp.pad(k, pad).reshape(B, nb + 2, SWA_BLOCK, SWA_KV_HEADS, SWA_HEAD_DIM)
    vp = jnp.pad(v, pad).reshape(B, nb + 2, SWA_BLOCK, SWA_KV_HEADS, SWA_HEAD_DIM)
    kb = jnp.concatenate([kp[:, :-2], kp[:, 1:-1], kp[:, 2:]], axis=2)
    vb = jnp.concatenate([vp[:, :-2], vp[:, 1:-1], vp[:, 2:]], axis=2)
    scores = jnp.einsum('bnqhgd,bnkhd->bnhgqk', qb, kb).astype(jnp.float32) * (SWA_HEAD_DIM ** -0.5)
    q_off = jnp.arange(SWA_BLOCK)[:, None]
    k_off = jnp.arange(3 * SWA_BLOCK)[None, :] - SWA_BLOCK
    band = jnp.abs(k_off - q_off) <= SWA_WINDOW
    k_pos = (jnp.arange(nb) * SWA_BLOCK)[:, None] + k_off
    valid = (k_pos >= 0) & (k_pos < S)
    mask = band[None, :, :] & valid[:, None, :]
    scores = jnp.where(mask[None, :, None, None], scores, NEG_INF)
    sink_l = jnp.broadcast_to(sink.astype(jnp.float32).reshape(1, 1, SWA_KV_HEADS, SWA_GROUP, 1, 1),
                              scores.shape[:-1] + (1,))
    probs = jax.nn.softmax(jnp.concatenate([scores, sink_l], axis=-1), axis=-1)[..., :-1]
    out = jnp.einsum('bnhgqk,bnkhd->bnqhgd', probs.astype(v.dtype), vb)
    return out.reshape(B, S, SWA_WIDTH)

def latent_attention(q_lat, kv_lat, k_rope_raw, q_norm, w_q_up, kv_norm, w_kv_up):
    B, S = q_lat.shape[0], q_lat.shape[1]
    nb = S // MLA_Q_BLOCK
    cos, sin = rope_tables(S, MLA_ROPE_DIM)
    q = (rmsnorm(q_lat, q_norm) @ w_q_up).reshape(B, S, MLA_HEADS, MLA_QK_DIM)
    q_nope = q[..., :MLA_NOPE_DIM]
    q_rope = apply_rope(q[..., MLA_NOPE_DIM:], cos, sin)
    kv = (rmsnorm(kv_lat, kv_norm) @ w_kv_up).reshape(B, S, MLA_HEADS, MLA_NOPE_DIM + MLA_V_DIM)
    k_nope = kv[..., :MLA_NOPE_DIM]
    v = kv[..., MLA_NOPE_DIM:]
    k_rope = apply_rope(k_rope_raw[:, :, None, :], cos, sin)[:, :, 0, :]
    scale = MLA_QK_DIM ** -0.5
    qn_blocks = q_nope.reshape(B, nb, MLA_Q_BLOCK, MLA_HEADS, MLA_NOPE_DIM).transpose(1, 0, 2, 3, 4)
    qr_blocks = q_rope.reshape(B, nb, MLA_Q_BLOCK, MLA_HEADS, MLA_ROPE_DIM).transpose(1, 0, 2, 3, 4)

    def attend(blk):
        qn, qr = blk
        s = (jnp.einsum('bqhd,bkhd->bhqk', qn, k_nope)
             + jnp.einsum('bqhd,bkd->bhqk', qr, k_rope)).astype(jnp.float32) * scale
        p = jax.nn.softmax(s, axis=-1).astype(v.dtype)
        return jnp.einsum('bhqk,bkhd->bqhd', p, v)

    out = lax.map(attend, (qn_blocks, qr_blocks))
    return out.transpose(1, 0, 2, 3, 4).reshape(B, S, MLA_WIDTH)

def peer(h, w_query, sub_keys, expert_u, expert_v):
    B, S, D = h.shape
    blocks = h.reshape((B * S) // PEER_TOKEN_BLOCK, PEER_TOKEN_BLOCK, D)

    def block(xb):
        q = (xb @ w_query).reshape(PEER_TOKEN_BLOCK, PEER_HEADS, 2, PEER_HALF_DIM)
        s = jnp.einsum('chpd,hpnd->chpn', q, sub_keys).astype(jnp.float32)
        top_s, top_i = lax.top_k(s, PEER_TOPK)
        cand_s = (top_s[:, :, 0, :, None] + top_s[:, :, 1, None, :]).reshape(
            PEER_TOKEN_BLOCK, PEER_HEADS, PEER_TOPK * PEER_TOPK)
        cand_i = (top_i[:, :, 0, :, None] * PEER_N_KEYS + top_i[:, :, 1, None, :]).reshape(
            PEER_TOKEN_BLOCK, PEER_HEADS, PEER_TOPK * PEER_TOPK)
        best_s, pos = lax.top_k(cand_s, PEER_TOPK)
        idx = jnp.take_along_axis(cand_i, pos, axis=-1)
        g = jax.nn.softmax(best_s, axis=-1)
        u = expert_u[idx]
        act = jax.nn.gelu(jnp.einsum('cd,chkd->chk', xb, u).astype(jnp.float32), approximate=False)
        w = (g * act).astype(xb.dtype)
        return jnp.einsum('chk,chkd->cd', w, expert_v[idx])

    return lax.map(block, blocks).reshape(B, S, D)

def first_inputs(seed: int = 0) -> dict:
    key = jax.random.key(seed)
    ks = jax.random.split(key, 20)
    f32 = jnp.float32
    nrm = lambda k, shape, s: jax.random.normal(k, shape, f32) * s
    L, D = DEPTH, D_MODEL
    return {
        "x": nrm(ks[0], (BATCH, SEQ, D), 1.0),
        "c": nrm(ks[1], (BATCH, D), 1.0),
        "w_ada": nrm(ks[2], (L, D, N_MOD * D), D ** -0.5),
        "b_ada": nrm(ks[3], (L, N_MOD * D), 0.01),
        "w_in": nrm(ks[4], (L, D, IN_WIDTH), D ** -0.5),
        "swa_sink": nrm(ks[5], (L, SWA_HEADS), 0.5),
        "mla_q_norm": 1.0 + nrm(ks[6], (L, MLA_Q_RANK), 0.02),
        "w_mla_q_up": nrm(ks[7], (L, MLA_Q_RANK, MLA_HEADS * MLA_QK_DIM), MLA_Q_RANK ** -0.5),
        "mla_kv_norm": 1.0 + nrm(ks[8], (L, MLA_KV_RANK), 0.02),
        "w_mla_kv_up": nrm(ks[9], (L, MLA_KV_RANK, MLA_HEADS * (MLA_NOPE_DIM + MLA_V_DIM)), MLA_KV_RANK ** -0.5),
        "out_norm_swa": 1.0 + nrm(ks[10], (L, SWA_WIDTH), 0.02),
        "out_norm_mla": 1.0 + nrm(ks[11], (L, MLA_WIDTH), 0.02),
        "w_out": nrm(ks[12], (L, MIX_WIDTH, D), MIX_WIDTH ** -0.5),
        "w_peer_query": nrm(ks[13], (L, D, PEER_HEADS * PEER_QUERY_DIM), D ** -0.5),
        "peer_sub_keys": nrm(ks[14], (L, PEER_HEADS, 2, PEER_N_KEYS, PEER_HALF_DIM), PEER_HALF_DIM ** -0.5),
        "peer_expert_u": nrm(ks[15], (L, PEER_EXPERTS, D), D ** -0.5),
        "peer_expert_v": nrm(ks[16], (L, PEER_EXPERTS, D), PEER_HEADS ** -0.5),
        "final_norm": 1.0 + nrm(ks[17], (D,), 0.02),
    }

def first_block(x, c, w_ada, b_ada, w_in, swa_sink, mla_q_norm, w_mla_q_up, mla_kv_norm, w_mla_kv_up,
              out_norm_swa, out_norm_mla, w_out, w_peer_query, peer_sub_keys, peer_expert_u,
              peer_expert_v, final_norm):
    B, S, D = x.shape
    c_act = jax.nn.silu(c)
    for l in range(DEPTH):
        mod = c_act @ w_ada[l] + b_ada[l]
        sh_a, sc_a, g_a, sh_f, sc_f, g_f = jnp.split(mod, N_MOD, axis=-1)

        h = modulate(rmsnorm(x), sh_a, sc_a)
        proj = h @ w_in[l]
        qa, ka, va, q_lat, kv_lat, k_rope_raw = jnp.split(proj, IN_SPLITS, axis=-1)
        o_a = windowed_gqa(qa.reshape(B, S, SWA_HEADS, SWA_HEAD_DIM),
                           ka.reshape(B, S, SWA_KV_HEADS, SWA_HEAD_DIM),
                           va.reshape(B, S, SWA_KV_HEADS, SWA_HEAD_DIM),
                           swa_sink[l])
        o_b = latent_attention(q_lat, kv_lat, k_rope_raw, mla_q_norm[l], w_mla_q_up[l],
                               mla_kv_norm[l], w_mla_kv_up[l])
        mixed = jnp.concatenate([rmsnorm(o_a, out_norm_swa[l]), rmsnorm(o_b, out_norm_mla[l])], axis=-1)
        x = x + g_a[:, None, :] * (mixed @ w_out[l])

        h = modulate(rmsnorm(x), sh_f, sc_f)
        x = x + g_f[:, None, :] * peer(h, w_peer_query[l], peer_sub_keys[l], peer_expert_u[l], peer_expert_v[l])
    return rmsnorm(x, final_norm)


HEAD_DIM = 64
N_Q_HEADS = 8
N_KV_HEADS = 2
Q_PER_KV = N_Q_HEADS // N_KV_HEADS
ATTN_WIDTH = N_Q_HEADS * HEAD_DIM
KV_WIDTH = N_KV_HEADS * HEAD_DIM
ROPE_PAIRS = HEAD_DIM // 4
Q_BLOCK = 128
POOL_WINDOWS = (2, 4, 8, 16)
N_POOL_GROUPS = len(POOL_WINDOWS)
POOL_WIDTH = D_MODEL - ATTN_WIDTH
POOL_GROUP_DIM = POOL_WIDTH // N_POOL_GROUPS
MIX_WIDTH_2 = ATTN_WIDTH + POOL_WIDTH
IN_WIDTH_2 = ATTN_WIDTH + 2 * KV_WIDTH + POOL_WIDTH
D_FF = ((8 * D_MODEL // 3 + 255) // 256) * 256
GRID_W = 64


def rmsnorm_2(x, g):
    xf = x.astype(jnp.float32)
    y = xf * lax.rsqrt(jnp.mean(xf * xf, axis=-1, keepdims=True) + EPS)
    return (y * g.astype(jnp.float32)).astype(x.dtype)

def rope_1d(x, ang):
    xf = x.astype(jnp.float32)
    x1, x2 = jnp.split(xf, 2, axis=-1)
    c = jnp.cos(ang)[None, :, None, :]
    s = jnp.sin(ang)[None, :, None, :]
    return jnp.concatenate([x1 * c - x2 * s, x2 * c + x1 * s], axis=-1).astype(x.dtype)

def axial_rope(x, ang_row, ang_col):
    xr, xc = jnp.split(x, 2, axis=-1)
    return jnp.concatenate([rope_1d(xr, ang_row), rope_1d(xc, ang_col)], axis=-1)

def attention_mixer(q, k, v, q_g, k_g, ang_row, ang_col):
    B, S, _ = q.shape
    q = q.reshape(B, S, N_Q_HEADS, HEAD_DIM)
    k = k.reshape(B, S, N_KV_HEADS, HEAD_DIM)
    v = v.reshape(B, S, N_KV_HEADS, HEAD_DIM)
    q = axial_rope(rmsnorm_2(q, q_g), ang_row, ang_col)
    k = axial_rope(rmsnorm_2(k, k_g), ang_row, ang_col)
    n_blk = S // Q_BLOCK
    qb = q.reshape(B, n_blk, Q_BLOCK, N_KV_HEADS, Q_PER_KV, HEAD_DIM).transpose(1, 0, 2, 3, 4, 5)
    scale = HEAD_DIM ** -0.5

    def block(qblk):
        s = jnp.einsum('bqkgd,bskd->bkgqs', qblk, k).astype(jnp.float32) * scale
        p = jax.nn.softmax(s, axis=-1)
        return jnp.einsum('bkgqs,bskd->bqkgd', p.astype(v.dtype), v)

    o = lax.map(block, qb)
    return o.transpose(1, 0, 2, 3, 4, 5).reshape(B, S, ATTN_WIDTH)

def pool_mixer(u, pool_w, pool_b, pool_scale):
    B, S, _ = u.shape
    ug = u.reshape(B, S, N_POOL_GROUPS, POOL_GROUP_DIM)
    uf = ug.astype(jnp.float32)
    csum = jnp.concatenate([jnp.zeros_like(uf[:, :1]), jnp.cumsum(uf, axis=1)], axis=1)
    t = jnp.arange(S)
    pooled = []
    for g, w in enumerate(POOL_WINDOWS):
        lo = jnp.clip(t - w // 2, 0, S)
        hi = jnp.clip(t - w // 2 + w, 0, S)
        cnt = (hi - lo).astype(jnp.float32)[None, :, None]
        cg = csum[:, :, g, :]
        mean = (cg[:, hi] - cg[:, lo]) / cnt
        pooled.append(mean - uf[:, :, g, :])
    pooled = jnp.stack(pooled, axis=1).astype(u.dtype)
    y = jnp.einsum('bgsc,gcd->bsgd', pooled, pool_w) + pool_b[None, None]
    return y.reshape(B, S, POOL_WIDTH) * pool_scale

def second_inputs(seed: int = 0) -> dict:
    key = jax.random.key(seed)
    ks = jax.random.split(key, 14)
    f32 = jnp.float32

    def nrm(k, shape, fan_in):
        return jax.random.normal(k, shape, f32) * fan_in ** -0.5

    def gain(k, shape):
        return 1.0 + 0.05 * jax.random.normal(k, shape, f32)

    res_scale = (2 * DEPTH) ** -0.5
    return {
        "x": jax.random.normal(ks[0], (BATCH, SEQ, D_MODEL), f32),
        "norm1_g": gain(ks[1], (DEPTH, D_MODEL)),
        "w_in": nrm(ks[2], (DEPTH, D_MODEL, IN_WIDTH_2), D_MODEL),
        "q_norm_g": gain(ks[3], (DEPTH, HEAD_DIM)),
        "k_norm_g": gain(ks[4], (DEPTH, HEAD_DIM)),
        "pool_w": nrm(ks[5], (DEPTH, N_POOL_GROUPS, POOL_GROUP_DIM, POOL_GROUP_DIM), POOL_GROUP_DIM),
        "pool_b": 0.02 * jax.random.normal(ks[6], (DEPTH, N_POOL_GROUPS, POOL_GROUP_DIM), f32),
        "pool_scale": gain(ks[7], (DEPTH, POOL_WIDTH)),
        "w_out": nrm(ks[8], (DEPTH, MIX_WIDTH_2, D_MODEL), MIX_WIDTH_2) * res_scale,
        "norm2_g": gain(ks[9], (DEPTH, D_MODEL)),
        "w_gate": nrm(ks[10], (DEPTH, D_MODEL, D_FF), D_MODEL),
        "w_up": nrm(ks[11], (DEPTH, D_MODEL, D_FF), D_MODEL),
        "w_down": nrm(ks[12], (DEPTH, D_FF, D_MODEL), D_FF) * res_scale,
    }

def second_block(x, norm1_g, w_in, q_norm_g, k_norm_g, pool_w, pool_b, pool_scale,
              w_out, norm2_g, w_gate, w_up, w_down):
    B, S, _ = x.shape
    rows = S // GRID_W
    row = jnp.repeat(jnp.arange(rows), GRID_W).astype(jnp.float32)
    col = (jnp.arange(S) % GRID_W).astype(jnp.float32)
    inv_freq = ROPE_THETA ** (-jnp.arange(ROPE_PAIRS, dtype=jnp.float32) / ROPE_PAIRS)
    ang_row = row[:, None] * inv_freq[None, :]
    ang_col = col[:, None] * inv_freq[None, :]

    splits = [ATTN_WIDTH, ATTN_WIDTH + KV_WIDTH, ATTN_WIDTH + 2 * KV_WIDTH]
    for l in range(DEPTH):
        h = rmsnorm_2(x, norm1_g[l])
        proj = h @ w_in[l]
        q, k, v, u = jnp.split(proj, splits, axis=-1)
        a = attention_mixer(q, k, v, q_norm_g[l], k_norm_g[l], ang_row, ang_col)
        p = pool_mixer(u, pool_w[l], pool_b[l], pool_scale[l])
        x = x + jnp.concatenate([a, p], axis=-1) @ w_out[l]
        h = rmsnorm_2(x, norm2_g[l])
        x = x + (jax.nn.silu(h @ w_gate[l]) * (h @ w_up[l])) @ w_down[l]
    return x


def setup_inputs(seed=0):
    out = dict(first_inputs(seed))
    for name, value in second_inputs(seed + 1).items():
        if name != "x":
            out[name + "_2"] = value
    return out


def reference(
    x, c, w_ada, b_ada, w_in, swa_sink, mla_q_norm, w_mla_q_up, mla_kv_norm, w_mla_kv_up,
    out_norm_swa, out_norm_mla, w_out, w_peer_query, peer_sub_keys, peer_expert_u,
    peer_expert_v, final_norm, norm1_g_2, w_in_2, q_norm_g_2, k_norm_g_2, pool_w_2, pool_b_2,
    pool_scale_2, w_out_2, norm2_g_2, w_gate_2, w_up_2, w_down_2,
):
    x = first_block(
        x, c, w_ada, b_ada, w_in, swa_sink, mla_q_norm, w_mla_q_up, mla_kv_norm, w_mla_kv_up,
        out_norm_swa, out_norm_mla, w_out, w_peer_query, peer_sub_keys, peer_expert_u,
        peer_expert_v, final_norm,
    )
    return second_block(
        x, norm1_g_2, w_in_2, q_norm_g_2, k_norm_g_2, pool_w_2, pool_b_2, pool_scale_2, w_out_2,
        norm2_g_2, w_gate_2, w_up_2, w_down_2,
    )


_drawn_inputs = setup_inputs


def setup_inputs(seed=0):
    import zlib

    import numpy as np

    out = dict(_drawn_inputs(seed))
    spreads = {}
    factors = {'b_ada': 2.761,
     'swa_sink': 8.0,
     'mla_q_norm': 8.0,
     'mla_kv_norm': 4.559,
     'out_norm_swa': 11.55,
     'out_norm_mla': 4.627,
     'final_norm': 2.718,
     'q_norm_g_2': 8.0,
     'k_norm_g_2': 8.0,
     'pool_b_2': 6.041,
     'pool_scale_2': 10.798,
     'norm2_g_2': 5.328}
    for name, (base, spread) in spreads.items():
        noise = np.random.default_rng([zlib.crc32(name.encode()), seed]).standard_normal(out[name].shape)
        drawn = base * np.exp(spread * noise) if base else spread * noise
        out[name] = __import__('jax').numpy.asarray(drawn.astype(out[name].dtype))
    for name, factor in factors.items():
        out[name] = (out[name] * factor).astype(out[name].dtype)
    return out
```

```python
from contextlib import ExitStack

import concourse.bass as bass
import numpy as np
from concourse import mybir

F32 = mybir.dt.float32
F32R = mybir.dt.float32r
U32 = mybir.dt.uint32
ALU = mybir.AluOpType
ACT = mybir.ActivationFunctionType
AX_X = mybir.AxisListType.X

P = 128
TOK = 512
TT = TOK // P
D = 1024
KD = D // P
EPS = 1e-6
SLOT = KD * P
THETA = 10000.0
WINDOW = 128
HD = 64
NH = 8
ROPE_D = 32
MLA_QK = HD + ROPE_D
SCALE = HD ** -0.5
MLA_SCALE = MLA_QK ** -0.5
NEG = -1e30
LOWEST = -3.0e38
TOPK = 16
NKEYS = 128
NPART = 16
FF = 2816
FB = FF // P
POOL_WINDOWS = (2, 4, 8, 16)
EARLY_R = 24
EARLY_G = 32
EARLY = EARLY_R + EARLY_G


def three_pass(pe, out, w_hi, w_lo, x_hi, x_lo, start, stop):
    pe.matmul(out, w_hi, x_hi, start=start, stop=False)
    pe.matmul(out, w_hi, x_lo, start=False, stop=False)
    return pe.matmul(out, w_lo, x_hi, start=False, stop=stop)


class Stream:
    def __init__(self, ctx, nc, tag, raw_slots, split_slots, items, last_block):
        self.R, self.Q = raw_slots, split_slots
        self.last_block = last_block
        self.raw = ctx.enter_context(nc.sbuf_tensor(tag + "_raw", [P, raw_slots, SLOT], F32))
        self.hi = ctx.enter_context(nc.sbuf_tensor(tag + "_hi", [P, split_slots, SLOT], F32R))
        self.lo = ctx.enter_context(nc.sbuf_tensor(tag + "_lo", [P, split_slots, SLOT], F32R))
        self.landed = [nc.alloc_semaphore(f"{tag}_landed{i}") for i in range(raw_slots)]
        self.hi_ready = nc.alloc_semaphore(tag + "_hi_ready")
        self.lo_ready = nc.alloc_semaphore(tag + "_lo_ready")
        self.projected = nc.alloc_semaphore(tag + "_projected")
        self.raw_used = nc.alloc_semaphore(tag + "_raw_used")
        self.pooled_used = nc.alloc_semaphore(tag + "_pooled_used")
        self.items = items
        self.where = []
        self.raws = []
        self.pooled = []
        for n, (kind, _, _) in enumerate(items):
            {"split": self.where, "raw": self.raws, "pooled": self.pooled}[kind].append(n)

    def wait_landed(self, eng, n):
        eng.wait_ge(self.landed[n % self.R], 16 * (n // self.R + 1))

    def loads(self, sp, first=0, last=None):
        for n in range(first, len(self.items) if last is None else last):
            kind, src, width = self.items[n]
            if n >= self.R:
                old = n - self.R
                if self.items[old][0] == "split":
                    sp.wait_ge(self.lo_ready, self.where.index(old) + 1)
                elif self.items[old][0] == "raw":
                    sp.wait_ge(self.raw_used, self.raws.index(old) + 1)
                else:
                    sp.wait_ge(self.pooled_used, self.pooled.index(old) + 1)
            sp.dma_start(self.raw[:, n % self.R, 0:width], src).then_inc(self.landed[n % self.R], 16)

    def split_hi(self, act, s):
        if s >= len(self.where):
            return
        n = self.where[s]
        w = self.items[n][2]
        self.wait_landed(act, n)
        if s >= self.Q:
            act.wait_ge(self.projected, self.last_block[s - self.Q] + 1)
        act.activation(self.hi[:, s % self.Q, 0:w], self.raw[:, n % self.R, 0:w], ACT.Copy).then_inc(self.hi_ready, 1)

    def split_lo(self, dve, s):
        if s >= len(self.where):
            return
        n = self.where[s]
        w = self.items[n][2]
        dve.wait_ge(self.hi_ready, s + 1)
        dve.tensor_tensor(self.lo[:, s % self.Q, 0:w], self.raw[:, n % self.R, 0:w],
                          self.hi[:, s % self.Q, 0:w].bitcast(F32), ALU.subtract).then_inc(self.lo_ready, 1)

    def weights(self, s, lo, hi):
        return self.hi[:, s % self.Q, lo:hi], self.lo[:, s % self.Q, lo:hi]


def dense_block(pe, st, s, out, x_hi, x_lo, nk=KD, x_ready=None):
    pe.wait_ge(st.lo_ready, s + 1)
    for k in range(nk):
        if x_ready is not None:
            pe.wait_ge(x_ready, k + 1)
        w_hi, w_lo = st.weights(s, k * P, k * P + P)
        mm = three_pass(pe, out, w_hi, w_lo, x_hi[:, k, :], x_lo[:, k, :], k == 0, k == nk - 1)
    return mm


class Norms:
    def __init__(self, ctx, nc, tag, bank, sq=None, rstd=None):
        self.sq = sq if sq is not None else ctx.enter_context(nc.sbuf_tensor(tag + "_sq", [P, 2, TOK], F32))
        self.rstd = rstd if rstd is not None else ctx.enter_context(nc.sbuf_tensor(tag + "_rstd", [P, 2, TOK], F32))
        self.bank = bank
        self.sq_ready = nc.alloc_semaphore(tag + "_sq_ready")
        self.summed = nc.alloc_semaphore(tag + "_summed")
        self.inv_ready = nc.alloc_semaphore(tag + "_inv_ready")
        self.rstd_ready = nc.alloc_semaphore(tag + "_rstd_ready")
        self.mean_ready = nc.alloc_semaphore(tag + "_mean_ready")

    def squares(self, act, first, sources):
        for n, src in enumerate(sources, first):
            if n >= 2:
                act.wait_ge(self.summed, n - 1)
            act.activation(self.sq[:, n % 2, :], src, ACT.Square).then_inc(self.sq_ready, 1)

    def sums(self, pe, ones, group, first, count):
        if group:
            pe.wait_ge(self.mean_ready, group)
        for n in range(first, first + count):
            pe.wait_ge(self.sq_ready, n + 1)
            pe.matmul(self.bank, ones, self.sq[:, n % 2, :], start=(n == first),
                      stop=(n == first + count - 1)).then_inc(self.summed, 1)

    def inverse(self, dve, group, upto, width):
        r = self.rstd[:, group % 2, :]
        dve.wait_ge(self.summed, upto)
        dve.tensor_scalar(r, self.bank, 1.0 / width, EPS, ALU.mult, ALU.add).then_inc(self.mean_ready, 1)
        dve.wait_ge(self.mean_ready, group + 1)
        dve.reciprocal(r, r).then_inc(self.inv_ready, 1)

    def root(self, act, group):
        r = self.rstd[:, group % 2, :]
        act.wait_ge(self.inv_ready, group + 1)
        act.activation(r, r, ACT.Sqrt).then_inc(self.rstd_ready, 1)


class Normed:
    def __init__(self, ctx, nc, tag):
        self.x = ctx.enter_context(nc.sbuf_tensor(tag + "_x", [P, 2, TOK], F32))
        self.full = ctx.enter_context(nc.sbuf_tensor(tag + "_full", [P, 2, TOK], F32))
        self.x_ready = nc.alloc_semaphore(tag + "_x_ready")
        self.full_ready = nc.alloc_semaphore(tag + "_full_ready")
        self.hi_done = nc.alloc_semaphore(tag + "_hi_done")
        self.lo_done = nc.alloc_semaphore(tag + "_lo_done")

    def dve(self, dve, first, x, rstd, gain, shift, hi, lo, blocks):
        def rest(n):
            dve.wait_ge(self.full_ready, n + 1)
            dve.wait_ge(self.hi_done, n + 1)
            dve.tensor_tensor(lo[:, n - first, :], self.full[:, n % 2, :], hi[:, n - first, :].bitcast(F32),
                              ALU.subtract).then_inc(self.lo_done, 1)
        for n in range(first, first + blocks):
            k = n - first
            if n >= 2:
                dve.wait_ge(self.lo_done, n - 1)
            if rstd is None:
                src = x(k)
            else:
                src = self.x[:, n % 2, :]
                dve.tensor_tensor(src, x(k), rstd, ALU.mult).then_inc(self.x_ready, 1)
            dve.wait_ge(self.x_ready, n + 1)
            if shift is None:
                ins = dve.tensor_scalar(self.full[:, n % 2, :], src, gain(k), None, ALU.mult)
            else:
                ins = dve.tensor_scalar(self.full[:, n % 2, :], src, gain(k), shift(k), ALU.mult, ALU.add)
            ins.then_inc(self.full_ready, 1)
            if k:
                rest(n - 1)
        rest(first + blocks - 1)

    def act(self, act, first, hi, blocks):
        for n in range(first, first + blocks):
            act.wait_ge(self.full_ready, n + 1)
            act.activation(hi[:, n - first, :], self.full[:, n % 2, :], ACT.Copy).then_inc(self.hi_done, 1)


class Rotation:
    def __init__(self, ctx, nc, tag, banks):
        self.banks = banks
        self.x = ctx.enter_context(nc.sbuf_tensor(tag + "_x", [P, 2, TOK], F32))
        self.t = ctx.enter_context(nc.sbuf_tensor(tag + "_t", [P, 2, 2, TOK], F32))
        self.paired = nc.alloc_semaphore(tag + "_paired")
        self.terms = nc.alloc_semaphore(tag + "_terms")
        self.done = nc.alloc_semaphore(tag + "_done")

    def pe(self, pe, n, pairing, ready, value):
        pe.wait_ge(ready, value)
        if n >= 2:
            pe.wait_ge(self.terms, 2 * (n - 2) + 2)
        pe.matmul(self.banks[n % 2], pairing, self.x[:, n % 2, :], start=True, stop=True).then_inc(self.paired, 1)

    def x_free(self, eng, n):
        if n >= 2:
            eng.wait_ge(self.paired, n - 1)
            eng.wait_ge(self.terms, 2 * (n - 2) + 1)

    def dve(self, dve, n, out, C, S, ready, value, rows=slice(0, P)):
        if n >= 2:
            dve.wait_ge(self.done, n - 1)
        dve.wait_ge(ready, value)
        dve.tensor_tensor(self.t[:, n % 2, 0, :], self.x[:, n % 2, :], C, ALU.mult).then_inc(self.terms, 1)
        dve.wait_ge(self.paired, n + 1)
        dve.tensor_tensor(self.t[:, n % 2, 1, :], self.banks[n % 2], S, ALU.mult).then_inc(self.terms, 1)
        dve.wait_ge(self.terms, 2 * n + 2)
        dve.tensor_tensor(out, self.t[rows, n % 2, 0, :], self.t[rows, n % 2, 1, :], ALU.add).then_inc(self.done, 1)


class Attention:
    LAG = 2

    def __init__(self, ctx, nc, tag, ps, units, ident, prob, probT, masked, outs, sinks):
        self.units, self.ident, self.outs, self.sinks = units, ident, outs, sinks
        self.prob, self.probT, self.masked = prob, probT, masked
        self.S = [ps[:, b, :] for b in (0, 1, 7)]
        self.PT = [ps[:, 2, :], ps[:, 3, :]]
        self.O = [ps[:, 4, :], ps[:, 5, :]]
        sb = lambda n, s: ctx.enter_context(nc.sbuf_tensor(f"{tag}_{n}", s, F32))
        sem = lambda n: nc.alloc_semaphore(f"{tag}_{n}")
        n = len(units)
        self.top, self.bias, self.sum, self.esink = sb("top", [P, n]), sb("bias", [P, n]), sb("sum", [P, n]), sb("esink", [P, n])
        self.scored, self.mask_done, self.top_done = sem("scored"), sem("mask_done"), sem("top_done")
        self.bias_done, self.exp_done, self.turned = sem("bias_done"), sem("exp_done"), sem("turned")
        self.kept_even, self.kept_odd = sem("kept_even"), sem("kept_odd")
        self.mixed, self.sink_less, self.sink_done, self.inv_step, self.out_done = (
            sem("mixed"), sem("sink_less"), sem("sink_done"), sem("inv_step"), sem("out_done"))
        self.n_sinks = sum(s is not None for s in sinks)

    def kept(self, eng, u):
        eng.wait_ge(self.kept_even, u // 2 + 1)
        if u:
            eng.wait_ge(self.kept_odd, (u + 1) // 2)

    def pe(self, pe, beside=None):
        n = len(self.units)
        for i in range(n + self.LAG + 1):
            if i < n:
                q, k = self.units[i][0:2]
                if i >= len(self.S):
                    pe.wait_ge(self.exp_done, i - len(self.S) + 1)
                pe.matmul(self.S[i % len(self.S)][:, 0:k.shape[-1]], q, k, start=True, stop=True).then_inc(self.scored, 1)
            if beside:
                beside(i)
            u = i - self.LAG
            if 0 <= u < n:
                keys = self.units[u][3]
                pe.wait_ge(self.exp_done, u + 1)
                if u >= 2:
                    self.kept(pe, u - 2)
                for j in range(len(keys)):
                    mm = pe.transpose(self.PT[u % 2][:, j * P:j * P + P], self.prob[u % len(self.prob)][:, j * P:j * P + P], self.ident)
                mm.then_inc(self.turned, 1)
            u = i - self.LAG - 1
            if u >= 0:
                v, keys = self.units[u][2:4]
                tile, head = divmod(u, NH)
                self.kept(pe, u)
                if head == 0 and tile >= 2:
                    pe.wait_ge(self.out_done, tile - 1)
                for j, key in enumerate(keys):
                    mm = pe.matmul(self.O[tile % 2][:, head * HD:(head + 1) * HD], self.probT[u % len(self.probT)][:, j * P:j * P + P],
                                   v(key), start=(j == 0), stop=(j == len(keys) - 1))
                mm.then_inc(self.mixed, 1)

    def keep(self, eng, u):
        w = len(self.units[u][3]) * P
        eng.wait_ge(self.turned, u + 1)
        if u >= len(self.probT):
            eng.wait_ge(self.mixed, u - len(self.probT) + 1)
        dst, src = self.probT[u % len(self.probT)][:, 0:w], self.PT[u % 2][:, 0:w]
        if u % 2:
            eng.activation(dst, src, ACT.Copy).then_inc(self.kept_odd, 1)
        else:
            eng.tensor_copy(dst, src).then_inc(self.kept_even, 1)

    def dve(self, dve):
        n = len(self.units)
        masks = steps = sunk = 0
        for i in range(n + self.LAG + 1 + NH):
            if i < n:
                _, k, _, keys, scale, mask = self.units[i]
                w = k.shape[-1]
                S = self.S[i % len(self.S)][:, 0:w]
                dve.wait_ge(self.scored, i + 1)
                if mask is not None:
                    if i >= len(self.masked):
                        dve.wait_ge(self.exp_done, i - len(self.masked) + 1)
                    masked = self.masked[i % len(self.masked)][:, 0:w]
                    dve.scalar_tensor_tensor(out=masked, in0=S, scalar=scale, in1=mask, op0=ALU.mult, op1=ALU.add).then_inc(self.mask_done, 1)
                    masks += 1
                    dve.wait_ge(self.mask_done, masks)
                    S = masked
                dve.reduce_max(self.top[:, i:i + 1], S, AX_X).then_inc(self.top_done, 1)
                dve.wait_ge(self.top_done, i + 1)
                tile, head = divmod(i, NH)
                top, bias = self.top[:, i:i + 1], self.bias[:, i:i + 1]
                if self.sinks[tile] is not None:
                    ins = dve.tensor_scalar(bias, top, self.sinks[tile][:, head:head + 1], -1.0, ALU.max, ALU.mult)
                else:
                    ins = dve.tensor_scalar(bias, top, -scale, None, ALU.mult)
                ins.then_inc(self.bias_done, 1)
                if head == NH - 1 and self.sinks[tile] is not None:
                    dve.wait_ge(self.bias_done, i + 1)
                    a = slice(i + 1 - NH, i + 1)
                    dve.tensor_tensor(self.esink[:, a], self.sinks[tile], self.bias[:, a], ALU.add).then_inc(self.sink_less, 1)
            u = i - self.LAG
            if 0 <= u < n and u % 2 == 0:
                self.keep(dve, u)
            u = i - self.LAG - 2
            if u >= 0 and u % NH == NH - 1 and u < n:
                tile = u // NH
                a = slice(u + 1 - NH, u + 1)
                total = self.sum[:, a]
                dve.wait_ge(self.exp_done, u + 1)
                if self.sinks[tile] is not None:
                    sunk += 1
                    dve.wait_ge(self.sink_done, sunk)
                    dve.tensor_tensor(total, total, self.esink[:, a], ALU.add).then_inc(self.inv_step, 1)
                    steps += 1
                    dve.wait_ge(self.inv_step, steps)
                dve.reciprocal(total, total).then_inc(self.inv_step, 1)
                steps += 1
                dve.wait_ge(self.inv_step, steps)
                dve.wait_ge(self.mixed, u + 1)
                dve.tensor_tensor(self.outs[tile], self.O[tile % 2].rearrange("p (h d) -> p h d", h=NH),
                                  total.unsqueeze(2).broadcast_to([P, NH, HD]), ALU.mult).then_inc(self.out_done, 1)

    def act(self, act):
        n = len(self.units)
        sunk = 0
        for i in range(n + self.LAG):
            if i < n:
                _, k, _, _, scale, mask = self.units[i]
                w = k.shape[-1]
                act.wait_ge(self.bias_done, i + 1)
                if i >= len(self.prob):
                    act.wait_ge(self.turned, i - len(self.prob) + 1)
                src = self.S[i % len(self.S)][:, 0:w] if mask is None else self.masked[i % len(self.masked)][:, 0:w]
                act.activation(self.prob[i % len(self.prob)][:, 0:w], src, ACT.Exp, bias=self.bias[:, i:i + 1],
                               scale=scale if mask is None else 1.0, accum_out=self.sum[:, i:i + 1]).then_inc(self.exp_done, 1)
                if i % NH == NH - 1 and self.sinks[i // NH] is not None:
                    sunk += 1
                    act.wait_ge(self.sink_less, sunk)
                    e = self.esink[:, i + 1 - NH:i + 1]
                    act.activation(e, e, ACT.Exp).then_inc(self.sink_done, 1)
            u = i - self.LAG
            if u >= 0 and u % 2:
                self.keep(act, u)


class Turn:
    def __init__(self, ctx, nc, tag, banks, ident):
        self.banks, self.ident = banks, ident
        self.turned = nc.alloc_semaphore(tag + "_turned")
        self.hi_done = nc.alloc_semaphore(tag + "_hi_done")
        self.lo_done = nc.alloc_semaphore(tag + "_lo_done")

    def pe(self, pe, n, source):
        if n >= 2:
            pe.wait_ge(self.lo_done, n - 1)
        for t in range(TT):
            mm = pe.transpose(self.banks[n % 2][:, t * P:t * P + P], source(t), self.ident)
        mm.then_inc(self.turned, 1)

    def act(self, act, n, hi, gain):
        act.wait_ge(self.turned, n + 1)
        act.activation(hi, self.banks[n % 2], ACT.Copy, scale=gain).then_inc(self.hi_done, 1)

    def dve(self, dve, n, lo, hi, gain):
        dve.wait_ge(self.hi_done, n + 1)
        dve.scalar_tensor_tensor(out=lo, in0=self.banks[n % 2], scalar=gain, in1=hi.bitcast(F32), op0=ALU.mult,
                                 op1=ALU.subtract).then_inc(self.lo_done, 1)


COLS = {}
_at = 0
for _name, _n in (("b_ada", 48), ("mla_q_norm", 2), ("mla_kv_norm", 1), ("out_norm", 8), ("final_norm", 8), ("norm1_g_2", 8),
                  ("q_gain", 1), ("k_gain", 1), ("pool_b", 4), ("pool_scale", 4), ("norm2_g_2", 8), ("c", 8)):
    COLS[_name] = _at
    _at += _n
NCOLS = _at
TABS = {}
_at = 0
for _name, _n in (("ident", P), ("ones", P), ("pair_swa", P), ("pair_mla", P), ("pair_ax", P), ("ones_heads", P), ("mask", 3 * P),
                  ("C_swa", TOK), ("S_swa", TOK), ("C_mla", TOK), ("S_mla", TOK), ("C_ax", TOK), ("S_ax", TOK), ("inv_cnt", 4 * TOK)):
    TABS[_name] = (_at, _n)
    _at += _n
NTABS = _at
SWA_UNITS = [(h, t) for t in range(TT) for h in range(NH)]


def turn_rows(t):
    return range(max(0, t - 1), min(TT, t + 2))


def mixer1(nc, ps, xT, cols, mod, ident, ones, col, modc, xT_d, cols_d, sink_d, tabs_d, w_ada_d, w_in_d, w_q_up_d,
           w_kv_up_d, w_out_d):
    ADA_A = 2 * KD
    QLAT, KVLAT, KROPE, K, Q0, V, UPQ, UPK, UPV, OUT = 0, 2, 3, 4, 5, 9, 10, 18, 22, 26
    ADA_POOL = [m for m in range(48) if m % 2 or m >= ADA_A]
    items = [("pooled" if m % 2 else "raw", w_ada_d[m], SLOT) for m in range(ADA_A)]
    items += [("split", w_in_d[m], SLOT) for m in range(10)]
    items += [("split", w_q_up_d[m], SLOT) for m in range(2)] + [("split", w_kv_up_d, SLOT)]
    items += [("pooled", w_ada_d[m], SLOT) for m in range(ADA_A, 48)]
    items += [("split", w_out_d[m], SLOT) for m in range(KD)]
    last_block = list(range(10)) + [UPQ + 3, UPQ + 7, UPV + 3] + [OUT + m for m in range(KD)]
    released = {j: s for s, j in enumerate(last_block)}
    OUT_SLOT = 13
    with nc.cleanup_on_exit(), ExitStack() as ctx:
        sb = lambda n, s, d=F32: ctx.enter_context(nc.sbuf_tensor("a_" + n, s, d))
        sem = lambda n: nc.alloc_semaphore("a_" + n)
        stream = Stream(ctx, nc, "a_w", 4, 2, items, last_block)
        projected = stream.projected
        norms = Norms(ctx, nc, "a_norms", ps[:, 7, :])
        normed = Normed(ctx, nc, "a_normed")
        rotation = Rotation(ctx, nc, "a_rot", [ps[:, 2, :], ps[:, 3, :]])
        turn = Turn(ctx, nc, "a_turn", [ps[:, 2, :], ps[:, 3, :]], ident[:])
        in_hi, in_lo = sb("in_hi", [P, KD, TOK], F32R), sb("in_lo", [P, KD, TOK], F32R)
        latn_hi, latn_lo = sb("latn_hi", [P, 3, TOK], F32R), sb("latn_lo", [P, 3, TOK], F32R)
        tables = ["pair_swa", "pair_mla", "mask", "C_swa", "S_swa", "C_mla", "S_mla"]
        tab = {n: sb(n, [P, TABS[n][1]]) for n in tables}
        sink = sb("sink", [P, NH])
        cact = sb("cact", [P, KD])
        product, partial = sb("product", [P, KD, P]), sb("partial", [P, 2, P])
        ada_halved, ada_quartered, ada_partial, ada_done = (sem("ada_halved"), sem("ada_quartered"), sem("ada_partial"),
                                                            sem("ada_done"))
        k_swa, q_swa, v_swa = sb("k_swa", [P, TOK]), sb("q_swa", [P, 4, TOK]), sb("v_swa", [P, TT, P])
        qh, kh, v_mla = sb("qh", [P, NH, TOK]), sb("kh", [P, NH, TOK]), sb("v_mla", [P, TT, TOK])
        o_tok = sb("o_tok", [P, 2, TT, TOK])
        lat = o_tok[:, 0, 0:3, :]
        k_rope = o_tok[:, 1, 0, :]
        ss = sb("ss", [P, 2 * TT])

        def x_rstd(k):
            return o_tok[:, k // TT, k % TT, :]

        square = rotation.t[:, 1, 1, :]
        loaded, cols_in, x_loaded, silu_done = sem("loaded"), sem("cols_in"), sem("x_loaded"), sem("silu_done")
        mod_step, kept, shared, ss_ready, ss_step = sem("mod_step"), sem("kept"), sem("shared"), sem("ss_ready"), sem("ss_step")
        root_done, scaled, added = sem("root_done"), sem("scaled"), sem("added")

        swa = []
        for h, t in SWA_UNITS:
            g, keys = h // 4, list(turn_rows(t))
            rows = slice(g * HD, g * HD + HD)
            m0 = (keys[0] - (t - 1)) * P
            swa.append((q_swa[rows, h % 4, t * P:t * P + P], k_swa[rows, keys[0] * P:(keys[-1] + 1) * P],
                        lambda key, g=g: v_swa[:, key, g * HD:g * HD + HD], keys, SCALE,
                        tab["mask"][:, m0:m0 + len(keys) * P]))
        mla = [(qh[0:MLA_QK, h, t * P:t * P + P], kh[0:MLA_QK, h, :], lambda key, h=h: v_mla[:, key, h * HD:h * HD + HD],
                list(range(TT)), MLA_SCALE, None) for h, t in SWA_UNITS]
        buffers = ([normed.x[:, 0, :], normed.x[:, 1, :], rotation.x[:, 0, :]],
                   [normed.full[:, 0, :], normed.full[:, 1, :], rotation.x[:, 1, :]],
                   [rotation.t[:, 0, 0, :], rotation.t[:, 0, 1, :], rotation.t[:, 1, 0, :]])
        outs = [o_tok[:, m, t, :].rearrange("p (h d) -> p h d", h=NH) for m in range(2) for t in range(TT)]
        attention = Attention(ctx, nc, "a_att", ps, swa + mla, ident[:], *buffers, outs, [sink[:]] * TT + [None] * TT)
        NLOADS = 2 + len(tables)

        with nc.Block() as block:
            @block.sync
            def _(sp):
                sp.dma_start(cols[:], cols_d).then_inc(cols_in, 16)
                stream.loads(sp, 0, 4)
                o, w = TABS["ones"]
                sp.dma_start(ones[:], tabs_d[:, o:o + w]).then_inc(x_loaded, 16)
                sp.dma_start(xT[:], xT_d).then_inc(x_loaded, 16)
                stream.loads(sp, 4, ADA_A + 2)
                sp.dma_start(sink[:], sink_d).then_inc(loaded, 16)
                for name, dst in [("ident", ident)] + list(tab.items()):
                    o, w = TABS[name]
                    sp.dma_start(dst[:], tabs_d[:, o:o + w]).then_inc(loaded, 16)
                stream.loads(sp, ADA_A + 2)

            @block.gpsimd
            def _(pool):
                pool.wait_ge(silu_done, 1)
                for a, m in enumerate(ADA_POOL):
                    n = stream.pooled[a]
                    stream.wait_landed(pool, n)
                    if a:
                        pool.wait_ge(ada_partial, a)
                    pool.tensor_tensor(product[:], stream.raw[:, n % stream.R, :].rearrange("p (k c) -> p k c", k=KD),
                                       cact[:].unsqueeze(2).broadcast_to([P, KD, P]), ALU.mult).then_inc(stream.pooled_used, 1)
                    pool.wait_ge(stream.pooled_used, a + 1)
                    pool.tensor_tensor(product[:, 0:4], product[:, 0:4], product[:, 4:8], ALU.add).then_inc(ada_halved, 1)
                    pool.wait_ge(ada_halved, a + 1)
                    pool.tensor_tensor(product[:, 0:2], product[:, 0:2], product[:, 2:4], ALU.add).then_inc(ada_quartered, 1)
                    pool.wait_ge(ada_quartered, a + 1)
                    if a >= 2:
                        pool.wait_ge(ada_done, a - 1)
                    pool.tensor_tensor(partial[:, a % 2, :], product[:, 0, :], product[:, 1, :], ALU.add).then_inc(ada_partial, 1)

            @block.tensor
            def _(pe):
                def ada(m):
                    if m in ADA_POOL:
                        a = ADA_POOL.index(m)
                        pe.wait_ge(ada_partial, a + 1)
                        pe.matmul(ps[:, 6, m:m + 1], partial[:, a % 2, :], ones[:, 0:1], start=True, stop=True).then_inc(ada_done, 1)
                        return
                    n = stream.raws[m // 2]
                    stream.wait_landed(pe, n)
                    for k in range(KD):
                        mm = pe.matmul(ps[:, 6, m:m + 1], stream.raw[:, n % stream.R, k * P:k * P + P], cact[:, k:k + 1],
                                       start=(k == 0), stop=(k == KD - 1))
                    mm.then_inc(stream.raw_used, 1)

                def bank(j):
                    if j >= 2:
                        if j == OUT:
                            pe.wait_ge(attention.exp_done, len(attention.units))
                        if j >= OUT + 2:
                            pe.wait_ge(added, j - OUT - 1)
                        elif j < OUT:
                            pe.wait_ge(kept, j - 1)
                    return ps[:, j % 2, :]

                pe.wait_ge(silu_done, 1)
                for m in range(0, ADA_A, 2):
                    ada(m)
                    if m == 2:
                        pe.wait_ge(x_loaded, 32)
                    if m >= 4:
                        ada(m - 3)
                    if m == ADA_A // 2:
                        norms.sums(pe, ones[:], 0, 0, KD)
                ada(ADA_A - 3)
                ada(ADA_A - 1)
                pe.wait_ge(loaded, 16 * NLOADS)
                for j in range(10):
                    if j == V:
                        out = bank(j)
                        pe.wait_ge(stream.lo_ready, j + 1)
                        for t in range(TT):
                            for k in range(KD):
                                w_hi, w_lo = stream.weights(j, k * P, k * P + P)
                                mm = three_pass(pe, out[:, t * P:t * P + P], in_hi[:, k, t * P:t * P + P],
                                                in_lo[:, k, t * P:t * P + P], w_hi, w_lo, k == 0, k == KD - 1)
                        mm.then_inc(projected, 1)
                    else:
                        dense_block(pe, stream, j, bank(j), in_hi, in_lo, x_ready=normed.lo_done if j == 0 else None).then_inc(projected, 1)
                    if j == K:
                        norms.sums(pe, ones[:], 1, KD, 2)
                    if j == Q0 + 2:
                        norms.sums(pe, ones[:], 2, KD + 2, 1)
                    if KROPE < j:
                        n = j - 1 - KROPE
                        rotation.pe(pe, n, tab["pair_mla" if n == 0 else "pair_swa"][:], kept, j)
                pe.wait_ge(normed.lo_done, KD + 3)
                for h in range(NH):
                    j = UPQ + h
                    out = bank(j)
                    s = 10 + h // 4
                    pe.wait_ge(stream.lo_ready, s + 1)
                    for k in range(2):
                        a = (h % 4) * 2 * P + k * P
                        w_hi, w_lo = stream.weights(s, a, a + P)
                        mm = three_pass(pe, out, w_hi, w_lo, latn_hi[:, k, :], latn_lo[:, k, :], k == 0, k == 1)
                    mm.then_inc(projected, 1)
                    if h:
                        rotation.pe(pe, 5 + h, tab["pair_mla"][:], kept, j)
                pe.wait_ge(stream.lo_ready, 13)
                for i in range(4):
                    j = UPK + i
                    w_hi, w_lo = stream.weights(12, i * P, i * P + P)
                    three_pass(pe, bank(j), w_hi, w_lo, latn_hi[:, 2, :], latn_lo[:, 2, :], True, True).then_inc(projected, 1)
                    if i == 0:
                        rotation.pe(pe, 13, tab["pair_mla"][:], kept, j)
                for t in range(TT):
                    j = UPV + t
                    w_hi, w_lo = stream.weights(12, TOK, 2 * TOK)
                    three_pass(pe, bank(j), latn_hi[:, 2, t * P:t * P + P], latn_lo[:, 2, t * P:t * P + P],
                               w_hi, w_lo, True, True).then_inc(projected, 1)
                pe.wait_ge(kept, OUT)
                pe.wait_ge(rotation.done, 14)
                pe.wait_ge(shared, 1)
                attention.pe(pe, lambda i: ada(ADA_A + i // 2) if i % 2 == 0 and ADA_A + i // 2 < 48 else None)
                for n in range(KD):
                    m, c = n // 4, (n % 4) * P
                    pe.wait_ge(scaled, TT * (m + 1))
                    turn.pe(pe, n, lambda t: o_tok[:, m, t, c:c + P])
                pe.wait_ge(turn.lo_done, KD)
                for m in range(KD):
                    dense_block(pe, stream, OUT_SLOT + m, bank(OUT + m), in_hi, in_lo).then_inc(projected, 1)

            @block.scalar
            def _(act):
                act.wait_ge(cols_in, 16)
                act.activation(cact[:], cols[:, COLS["c"]:COLS["c"] + KD], ACT.Silu).then_inc(silu_done, 1)
                act.wait_ge(x_loaded, 32)
                norms.squares(act, 0, [xT[:, k, :] for k in range(KD)])
                norms.root(act, 0)
                normed.act(act, 0, in_hi, KD)
                stream.split_hi(act, 0)
                stream.split_hi(act, 1)
                for j in range(OUT):
                    act.wait_ge(projected, j + 1)
                    src = ps[:, j % 2, :]
                    if j < KROPE:
                        ins = act.activation(lat[:, j, :], src, ACT.Copy)
                    elif j < V or UPQ <= j < UPK:
                        n = j - KROPE if j < V else j - UPQ + 6
                        rotation.x_free(act, n)
                        ins = act.activation(rotation.x[:, n % 2, :], src, ACT.Copy)
                    elif j == V:
                        ins = act.activation(v_swa[:], src.rearrange("p (t c) -> p t c", t=TT), ACT.Copy)
                    elif j < UPV:
                        i = j - UPK
                        act.activation(kh[0:HD, 2 * i, :], src[0:HD, :], ACT.Copy)
                        ins = act.activation(kh[0:HD, 2 * i + 1, :], src[HD:P, :], ACT.Copy)
                    else:
                        ins = act.activation(v_mla[:, j - UPV, :], src, ACT.Copy)
                    ins.then_inc(kept, 1)
                    if j in released and released[j] + stream.Q < OUT_SLOT:
                        stream.split_hi(act, released[j] + stream.Q)
                    if j == KVLAT:
                        act.wait_ge(kept, KVLAT + 1)
                        norms.squares(act, KD, [lat[:, i, :] for i in range(3)])
                    if j == V:
                        norms.root(act, 1)
                        norms.root(act, 2)
                        normed.act(act, KD, latn_hi, 2)
                        normed.act(act, KD + 2, latn_hi[:, 2:3, :], 1)
                        act.wait_ge(rotation.done, 1)
                        act.activation(kh[HD:MLA_QK, :, :], k_rope[HD:MLA_QK, :].rearrange("p (a n) -> p a n", a=1)
                                       .broadcast_to([ROPE_D, NH, TOK]), ACT.Copy).then_inc(shared, 1)
                attention.act(act)
                stream.split_hi(act, OUT_SLOT)
                stream.split_hi(act, OUT_SLOT + 1)
                act.wait_ge(attention.out_done, 2 * TT)
                for i in range(2 * TT):
                    if i:
                        act.wait_ge(ss_ready, i)
                    act.activation(square, o_tok[:, i // TT, i % TT, :], ACT.Square, accum_out=ss[:, i:i + 1]).then_inc(ss_ready, 1)
                act.wait_ge(ss_step, 2)
                act.activation(ss[:], ss[:], ACT.Sqrt).then_inc(root_done, 1)
                for n in range(KD):
                    turn.act(act, n, in_hi[:, n, :], col("out_norm", n))
                for m in range(KD):
                    if m:
                        stream.split_hi(act, OUT_SLOT + m - 1 + stream.Q)

            @block.vector
            def _(dve):
                norms.inverse(dve, 0, KD, D)
                dve.wait_ge(norms.rstd_ready, 1)
                for k in range(KD):
                    dve.tensor_tensor(x_rstd(k), xT[:, k, :], norms.rstd[:, 0, :], ALU.mult).then_inc(normed.x_ready, 1)
                dve.wait_ge(stream.raw_used, ADA_A // 2)
                dve.wait_ge(ada_done, ADA_A // 2)
                dve.tensor_tensor(mod[:, 0:ADA_A], ps[:, 6, 0:ADA_A], cols[:, 0:ADA_A], ALU.add).then_inc(mod_step, 1)
                dve.wait_ge(mod_step, 1)
                dve.tensor_scalar(mod[:, KD:2 * KD], mod[:, KD:2 * KD], 1.0, None, ALU.add).then_inc(mod_step, 1)
                dve.wait_ge(mod_step, 2)
                normed.dve(dve, 0, x_rstd, None, lambda k: modc(1, k), lambda k: modc(0, k),
                           in_hi, in_lo, KD)
                stream.split_lo(dve, 0)
                stream.split_lo(dve, 1)
                dve.wait_ge(loaded, 16 * NLOADS)
                for j in range(OUT):
                    if j in released and released[j] + stream.Q < OUT_SLOT:
                        stream.split_lo(dve, released[j] + stream.Q)
                    if KROPE < j < UPQ:
                        n = j - 1 - KROPE
                        out = k_rope if n == 0 else k_swa[:] if n == 1 else q_swa[:, n - 2, :]
                        C, S = ("C_mla", "S_mla") if n == 0 else ("C_swa", "S_swa")
                        rotation.dve(dve, n, out, tab[C][:], tab[S][:], kept, j)
                    if UPQ < j <= UPK:
                        n = 5 + j - UPQ
                        rotation.dve(dve, n, qh[0:MLA_QK, n - 6, :], tab["C_mla"][:], tab["S_mla"][:], kept, j, slice(0, MLA_QK))
                    if j == Q0:
                        norms.inverse(dve, 1, KD + 2, 2 * P)
                    if j == V:
                        norms.inverse(dve, 2, KD + 3, P)
                        dve.wait_ge(norms.rstd_ready, 2)
                        normed.dve(dve, KD, lambda k: lat[:, k, :], norms.rstd[:, 1, :], lambda k: col("mla_q_norm", k), None,
                                   latn_hi, latn_lo, 2)
                        dve.wait_ge(norms.rstd_ready, 3)
                        normed.dve(dve, KD + 2, lambda k: lat[:, 2, :], norms.rstd[:, 0, :], lambda k: col("mla_kv_norm"), None,
                                   latn_hi[:, 2:3, :], latn_lo[:, 2:3, :], 1)
                dve.wait_ge(shared, 1)
                attention.dve(dve)
                dve.wait_ge(ada_done, len(ADA_POOL))
                dve.tensor_tensor(mod[:, ADA_A:48], ps[:, 6, ADA_A:48], cols[:, ADA_A:48], ALU.add).then_inc(mod_step, 1)
                dve.wait_ge(mod_step, 3)
                dve.tensor_scalar(mod[:, 4 * KD:5 * KD], mod[:, 4 * KD:5 * KD], 1.0, None, ALU.add).then_inc(mod_step, 1)
                dve.wait_ge(ss_ready, 2 * TT)
                dve.tensor_scalar(ss[:], ss[:], 1.0 / TOK, EPS, ALU.mult, ALU.add).then_inc(ss_step, 1)
                dve.wait_ge(ss_step, 1)
                dve.reciprocal(ss[:], ss[:]).then_inc(ss_step, 1)
                dve.wait_ge(root_done, 1)
                for i in range(2 * TT):
                    o = o_tok[:, i // TT, i % TT, :]
                    dve.tensor_scalar(o, o, ss[:, i:i + 1], None, ALU.mult).then_inc(scaled, 1)
                stream.split_lo(dve, OUT_SLOT)
                stream.split_lo(dve, OUT_SLOT + 1)
                for n in range(KD):
                    turn.dve(dve, n, in_lo[:, n, :], in_hi[:, n, :], col("out_norm", n))
                for m in range(KD):
                    if m:
                        stream.split_lo(dve, OUT_SLOT + m - 1 + stream.Q)
                    dve.wait_ge(projected, OUT + m + 1)
                    dve.scalar_tensor_tensor(out=xT[:, m, :], in0=ps[:, m % 2, :], scalar=modc(2, m), in1=xT[:, m, :],
                                             op0=ALU.mult, op1=ALU.add).then_inc(added, 1)


def program(nc, xT_d, cols_d, sink_d, tabs_d, w_ada_d, w_in_d, w_q_up_d, w_kv_up_d, w_out_d, w_query_d, keys_d,
            U_d, V_d, w_in2_d, pool_w_d, w_out2_d, w_gu_d, w_down_d, out_d):
    G_d = nc.dram_tensor("gates", (P, NKEYS, TOK), F32, kind="Internal").ap()
    early_d = nc.dram_tensor("early", (EARLY, P, TOK), F32, kind="Internal").ap()
    x_d = nc.dram_tensor("x_kept", (P, KD, TOK), F32, kind="Internal").ap()
    with ExitStack() as ctx:
        ps = ctx.enter_context(nc.psum_tensor("ps", [P, 8, TOK], F32))
        xT = ctx.enter_context(nc.sbuf_tensor("xT", [P, KD, TOK], F32))
        cols = ctx.enter_context(nc.sbuf_tensor("cols", [P, NCOLS], F32))
        mod = ctx.enter_context(nc.sbuf_tensor("mod", [P, 48], F32))
        ident = ctx.enter_context(nc.sbuf_tensor("ident", [P, P], F32))
        ones = ctx.enter_context(nc.sbuf_tensor("ones", [P, P], F32))

        def col(name, k=0):
            return cols[:, COLS[name] + k:COLS[name] + k + 1]

        def modc(part, k):
            return mod[:, part * KD + k:part * KD + k + 1]

        mixer1(nc, ps, xT, cols, mod, ident, ones, col, modc, xT_d, cols_d, sink_d, tabs_d, w_ada_d, w_in_d, w_q_up_d,
               w_kv_up_d, w_out_d)
        with ExitStack() as peer:
            h_hi = peer.enter_context(nc.sbuf_tensor("h_hi", [P, KD, TOK], F32R))
            h_lo = peer.enter_context(nc.sbuf_tensor("h_lo", [P, KD, TOK], F32R))
            with ExitStack() as routed:
                choice = [routed.enter_context(nc.sbuf_tensor(n, [P, TOK], F32)) for n in ("choice_i", "choice_j", "choice_g")]
                routing(nc, ps, xT, h_hi, h_lo, ident, ones, modc, w_query_d, keys_d, choice, U_d, early_d, x_d)
                gates(nc, ps, xT, h_hi, h_lo, choice, G_d, U_d, early_d)
            y = peer.enter_context(nc.sbuf_tensor("y", [P, KD, TOK], F32))
            early(nc, ps, xT, y, V_d, G_d, early_d, x_d)
            experts(nc, ps, xT, y, h_hi, h_lo, ones, col, modc, U_d, V_d, G_d)
        mixer2(nc, ps, xT, ident, ones, col, tabs_d, w_in2_d, pool_w_d, w_out2_d)
        swiglu(nc, ps, xT, ones, col, w_gu_d, w_down_d, out_d)


def routing(nc, ps, xT, h_hi, h_lo, ident, ones, modc, w_query_d, keys_d, choice, U_d, early_d, x_d):
    items = [("split", w_query_d[m], SLOT) for m in range(NPART)] + [("split", U_d[n], SLOT) for n in range(EARLY_R)]
    BLOCKS = NPART + EARLY_R
    with nc.cleanup_on_exit(), ExitStack() as ctx:
        sb = lambda n, s, d=F32: ctx.enter_context(nc.sbuf_tensor("r_" + n, s, d))
        sem = lambda n: nc.alloc_semaphore("r_" + n)
        stream = Stream(ctx, nc, "r_w", 4, 2, items, list(range(BLOCKS)))
        projected = stream.projected
        norms = Norms(ctx, nc, "r_norms", ps[:, 7, :])
        normed = Normed(ctx, nc, "r_normed")
        keys = sb("keys", [P, NPART, NKEYS])
        q = sb("q", [P, 2, TOK])
        rest = sb("rest", [P, TT, NKEYS])
        top = sb("top", [P, TT, NPART, TOPK])
        topi = sb("topi", [P, TT, NPART, TOPK], U32)
        topf = sb("topf", [P, TT, NPART, TOPK])
        cand = sb("cand", [P, NH, TOPK * TOPK])
        cand_rest = sb("cand_rest", [P, NH, TOPK * TOPK])
        best = sb("best", [P, TT, NH, TOPK])
        pos = sb("pos", [P, NH * TOPK], U32)
        half = sb("half", [P, 2, NH * TOPK], U32)
        halff = sb("halff", [P, 2, NH * TOPK])
        pick = sb("pick", [P, NH * TOPK, TOPK])
        total = sb("total", [P, TT * NH])
        tok = sb("tok", [P, 3, TT, NH * TOPK])
        iota = sb("iota", [P, TOPK])
        keys_in, kept, scored, picked, step = sem("keys_in"), sem("kept"), sem("scored"), sem("picked"), sem("step")
        iota_done, less_done, exp_done, tok_done, turned, laid = (sem("iota_done"), sem("less_done"), sem("exp_done"),
                                                                sem("tok_done"), sem("turned"), sem("laid"))
        early_out, x_kept = [sem("early_out0"), sem("early_out1")], sem("x_kept")
        PICKS = 5 * TT

        with nc.Block() as block:
            @block.sync
            def _(sp):
                stream.loads(sp, 0, 4)
                sp.dma_start(keys[:], keys_d).then_inc(keys_in, 16)
                sp.dma_start(x_d, xT[:]).then_inc(x_kept, 16)
                stream.loads(sp, 4)
                sp.wait_ge(x_kept, 16)

            @block.gpsimd
            def _(pool):
                pool.iota(iota[:], [[1, TOPK]], base=0, channel_multiplier=0,
                          allow_small_or_imprecise_dtypes=True).then_inc(iota_done, 1)
                for e in range(EARLY_R):
                    n = NPART + e
                    pool.wait_ge(kept, n + 1)
                    pool.dma_start(early_d[e], q[:, n % 2, :]).then_inc(early_out[e % 2], 16)
                    if n + stream.Q < BLOCKS:
                        pool.wait_ge(stream.lo_ready, n + stream.Q)
                        stream.split_lo(pool, n + stream.Q)
                for b in range(2):
                    pool.wait_ge(early_out[b], 16 * (EARLY_R // 2))

            @block.tensor
            def _(pe):
                norms.sums(pe, ones[:], 0, 0, KD)
                pe.wait_ge(keys_in, 16)

                def scores(n):
                    pe.wait_ge(kept, n + 1)
                    if n >= 2:
                        pe.wait_ge(picked, PICKS * (n - 2) + 3 * TT)
                    for t in range(TT):
                        mm = pe.matmul(ps[:, 2 + n % 2, t * NKEYS:(t + 1) * NKEYS], q[:, n % 2, t * P:t * P + P],
                                       keys[:, n, :], start=True, stop=True)
                    mm.then_inc(scored, 1)

                for n in range(NPART):
                    if n >= 2:
                        pe.wait_ge(kept, n - 1)
                    dense_block(pe, stream, n, ps[:, n % 2, :], h_hi, h_lo, x_ready=normed.lo_done if n == 0 else None).then_inc(projected, 1)
                    if n:
                        scores(n - 1)
                scores(NPART - 1)
                for n in range(NPART, BLOCKS):
                    pe.wait_ge(kept, n - 1)
                    dense_block(pe, stream, n, ps[:, n % 2, :], h_hi, h_lo).then_inc(projected, 1)
                pe.wait_ge(tok_done, 3)
                for x in range(3):
                    for t in range(TT):
                        mm = pe.transpose(ps[:, 4 + x, t * P:t * P + P], tok[:, x, t, :], ident[:])
                    mm.then_inc(turned, 1)

            @block.scalar
            def _(act):
                norms.squares(act, 0, [xT[:, k, :] for k in range(KD)])
                stream.split_hi(act, 0)
                stream.split_hi(act, 1)
                norms.root(act, 0)
                normed.act(act, 0, h_hi, KD)
                for n in range(NPART):
                    act.wait_ge(projected, n + 1)
                    if n >= 2:
                        act.wait_ge(scored, n - 1)
                    act.activation(q[:, n % 2, :], ps[:, n % 2, :], ACT.Copy).then_inc(kept, 1)
                    stream.split_hi(act, n + stream.Q)
                for e in range(EARLY_R):
                    n = NPART + e
                    act.wait_ge(projected, n + 1)
                    if e < 2:
                        act.wait_ge(scored, n - 1)
                    else:
                        act.wait_ge(early_out[e % 2], 16 * (e // 2))
                    act.activation(q[:, n % 2, :], ps[:, n % 2, :], ACT.Gelu).then_inc(kept, 1)
                    stream.split_hi(act, n + stream.Q)
                act.wait_ge(less_done, 1)
                act.activation(best[:], best[:], ACT.Exp).then_inc(exp_done, 1)
                for x in range(3):
                    act.wait_ge(turned, x + 1)
                    act.activation(choice[x][:], ps[:, 4 + x, :], ACT.Copy).then_inc(laid, 1)

            @block.vector
            def _(dve):
                steps = [0]

                def link(ins):
                    steps[0] += 1
                    ins.then_inc(step, 1)
                    dve.wait_ge(step, steps[0])

                norms.inverse(dve, 0, KD, D)
                stream.split_lo(dve, 0)
                stream.split_lo(dve, 1)
                dve.wait_ge(norms.rstd_ready, 1)
                normed.dve(dve, 0, lambda k: xT[:, k, :], norms.rstd[:, 0, :], lambda k: modc(4, k), lambda k: modc(3, k),
                           h_hi, h_lo, KD)
                for n in range(NPART):
                    stream.split_lo(dve, n + stream.Q)
                    dve.wait_ge(scored, n + 1)
                    S = [ps[:, 2 + n % 2, t * NKEYS:(t + 1) * NKEYS] for t in range(TT)]
                    done = PICKS * n
                    for t in range(TT):
                        dve.max(top[:, t, n, 0:8], S[t]).then_inc(picked, 1)
                    dve.wait_ge(picked, done + TT)
                    for t in range(TT):
                        dve.max_index(topi[:, t, n, 0:8], top[:, t, n, 0:8], S[t]).then_inc(picked, 1)
                        dve.match_replace(rest[:, t, :], top[:, t, n, 0:8], S[t], LOWEST).then_inc(picked, 1)
                    dve.wait_ge(picked, done + 3 * TT)
                    for t in range(TT):
                        dve.max(top[:, t, n, 8:16], rest[:, t, :]).then_inc(picked, 1)
                    dve.wait_ge(picked, done + 4 * TT)
                    for t in range(TT):
                        dve.max_index(topi[:, t, n, 8:16], top[:, t, n, 8:16], rest[:, t, :]).then_inc(picked, 1)
                    dve.wait_ge(picked, done + 5 * TT)
                dve.wait_ge(iota_done, 1)
                link(dve.tensor_copy(topf[:], topi[:]))
                for t in range(TT):
                    halves = top[:, t, :, :].rearrange("p (h s) a -> p h s a", s=2)
                    shape = [P, NH, TOPK, TOPK]
                    link(dve.tensor_tensor(cand[:].rearrange("p h (a b) -> p h a b", a=TOPK),
                                           halves[:, :, 0, :].unsqueeze(3).broadcast_to(shape),
                                           halves[:, :, 1, :].unsqueeze(2).broadcast_to(shape), ALU.add))
                    for h in range(NH):
                        last = dve.max(best[:, t, h, 0:8], cand[:, h, :])
                    link(last)
                    for h in range(NH):
                        dve.max_index(pos[:, h * TOPK:h * TOPK + 8], best[:, t, h, 0:8], cand[:, h, :])
                        last = dve.match_replace(cand_rest[:, h, :], best[:, t, h, 0:8], cand[:, h, :], LOWEST)
                    link(last)
                    for h in range(NH):
                        last = dve.max(best[:, t, h, 8:16], cand_rest[:, h, :])
                    link(last)
                    for h in range(NH):
                        last = dve.max_index(pos[:, h * TOPK + 8:(h + 1) * TOPK], best[:, t, h, 8:16], cand_rest[:, h, :])
                    link(last)
                    dve.tensor_scalar(half[:, 0, :], pos[:], 4, None, ALU.logical_shift_right)
                    link(dve.tensor_scalar(half[:, 1, :], pos[:], TOPK - 1, None, ALU.bitwise_and))
                    link(dve.tensor_copy(halff[:], half[:]))
                    for s in range(2):
                        shape = [P, NH * TOPK, TOPK]
                        link(dve.tensor_tensor(pick[:], halff[:, s, :].unsqueeze(2).broadcast_to(shape),
                                               iota[:].unsqueeze(1).broadcast_to(shape), ALU.is_equal))
                        four = pick[:].rearrange("p (h k) a -> p h k a", h=NH)
                        names = topf[:, t, :, :].rearrange("p (h s) a -> p h s a", s=2)[:, :, s, :]
                        link(dve.tensor_tensor(four, four, names.unsqueeze(2).broadcast_to([P, NH, TOPK, TOPK]), ALU.mult))
                        ins = dve.reduce_sum(tok[:, s, t, :], pick[:], AX_X)
                        if t < TT - 1:
                            link(ins)
                        else:
                            ins.then_inc(tok_done, 1)
                            dve.wait_ge(tok_done, s + 1)
                groups = best[:].rearrange("p t h k -> p (t h) k")
                shape = [P, TT * NH, TOPK]
                link(dve.tensor_copy(total[:], groups[:, :, 0]))
                dve.tensor_tensor(groups, groups, total[:].unsqueeze(2).broadcast_to(shape), ALU.subtract).then_inc(less_done, 1)
                dve.wait_ge(exp_done, 1)
                link(dve.reduce_sum(total[:], groups, AX_X))
                link(dve.reciprocal(total[:], total[:]))
                dve.tensor_tensor(tok[:, 2, :, :].rearrange("p t (h k) -> p (t h) k", h=NH), groups,
                                  total[:].unsqueeze(2).broadcast_to(shape), ALU.mult).then_inc(tok_done, 1)


def gates(nc, ps, xT, h_hi, h_lo, choice, G_d, U_d, early_d):
    BATCH, QUARTER = 4, SLOT // 4
    STEPS = TOK // (4 * BATCH)
    PARTS = 8
    assert STEPS == EARLY_G
    with nc.cleanup_on_exit(), ExitStack() as ctx:
        sb = lambda n, s, d=F32: ctx.enter_context(nc.sbuf_tensor("g_" + n, s, d))
        sem = lambda n: nc.alloc_semaphore("g_" + n)
        iota = sb("iota", [P, NKEYS])
        hot_i = sb("hot_i", [P, 2, BATCH, NKEYS])
        hot_j = xT[:, 6:8, :].rearrange("p b (c n) -> p b c n", c=BATCH)
        dense = sb("dense", [P, 2, NKEYS, P])
        u_hi, u_lo = sb("u_hi", [P, 2, SLOT], F32R), sb("u_lo", [P, 2, SLOT], F32R)
        u_raw = xT[:, 0:4, :].rearrange("p (r a) n -> p r (a n)", r=2)
        result = xT[:, 4:6, :]
        iota_done, eq_done, hot_done = sem("iota_done"), sem("eq_done"), sem("hot_done")
        u_in, stored, early_out = [sem("u_in0"), sem("u_in1")], [sem("stored0"), sem("stored1")], sem("early_out")
        hi_done, lo_done = sem("hi_done"), sem("lo_done")
        used, kept, a_done, gelu_done, result_free = sem("used"), sem("kept"), sem("a_done"), sem("gelu_done"), sem("result_free")
        HOT_FREE, BANK_FREE, U_FREE, A_FREE, RESULT_FREE = 2, 4, 8, 2, 2
        AHEAD, ROUNDED = 4, 5

        with nc.Block() as block:
            @block.gpsimd
            def _(pool):
                def load(tile, r):
                    pool.dma_start(u_raw[:, r, :], U_d[bass.ds(tile + EARLY_R, 1)].rearrange("o p n -> p (o n)")).then_inc(u_in[r], 16)

                def step(s, r):
                    pool.wait_ge(lo_done, 4 * s + 4)
                    load(s + 2, r)
                    pool.wait_ge(gelu_done, s + (A_FREE + 1))
                    pool.dma_start(early_d[bass.ds(s + EARLY_R, 1)].rearrange("o p n -> p (o n)"), result[:, r, :]).then_inc(early_out, 16)
                    pool.wait_ge(early_out, 16 * s + 16)
                    pool.sem_inc(result_free, 1)

                load(0, 0)
                load(1, 1)
                pool.sem_inc(result_free, RESULT_FREE)
                pool.iota(iota[:], [[1, NKEYS]], base=0, channel_multiplier=0,
                          allow_small_or_imprecise_dtypes=True).then_inc(iota_done, 1)
                with pool.Fori(0, STEPS // 2) as i:
                    step(2 * i, 0)
                    step(2 * i + 1, 1)

            @block.vector
            def _(dve):
                def rest(L, q, r):
                    a = slice(q * QUARTER, (q + 1) * QUARTER)
                    dve.wait_ge(hi_done, L + 1)
                    dve.tensor_tensor(u_lo[:, r, a], u_raw[:, r, a], u_hi[:, r, a].bitcast(F32), ALU.subtract).then_inc(lo_done, 1)

                for q in range(AHEAD):
                    rest(q, q, 0)
                dve.wait_ge(iota_done, 1)
                shape = [P, BATCH, NKEYS]
                names = iota[:].unsqueeze(1).broadcast_to(shape)
                with dve.Fori(0, STEPS // 2) as i:
                    for e in range(2):
                        for b in range(4):
                            B = 8 * i + (4 * e + b)

                            def of(x):
                                return choice[x][:, bass.ds(B * BATCH, BATCH)].unsqueeze(2).broadcast_to(shape)
                            dve.wait_ge(used, B + 1)
                            dve.tensor_tensor(hot_j[:, b % 2], names, of(1), ALU.is_equal).then_inc(eq_done, 1)
                            dve.tensor_tensor(hot_i[:, b % 2], names, of(0), ALU.is_equal)
                            dve.wait_ge(eq_done, B + 1)
                            dve.tensor_tensor(hot_j[:, b % 2], hot_j[:, b % 2], of(2), ALU.mult).then_inc(hot_done, 1)
                            rest(B + AHEAD, (b + AHEAD) % 4, (e + (b + AHEAD) // 4) % 2)

            @block.tensor
            def _(pe):
                pe.sem_inc(used, HOT_FREE)
                pe.sem_inc(a_done, U_FREE)
                with pe.Fori(0, STEPS // 2) as i:
                    for e in range(2):
                        for b in range(4):
                            B = 8 * i + (4 * e + b)
                            pe.wait_ge(hot_done, B + 1)
                            pe.wait_ge(kept, B + 1)
                            for c in range(BATCH):
                                mm = pe.matmul(ps[:, b, c * NKEYS:(c + 1) * NKEYS], hot_i[:, b % 2, c, :], hot_j[:, b % 2, c, :],
                                               start=True, stop=True)
                            mm.then_inc(used, 1)
                            pe.wait_ge(lo_done, B + 1)
                            if b == 0:
                                pe.wait_ge(gelu_done, 2 * i + (e + 1))
                            for k in (2 * b, 2 * b + 1):
                                a = slice(k * P, k * P + P)
                                mm = three_pass(pe, ps[:, 4 + e, :], u_hi[:, e, a], u_lo[:, e, a], h_hi[:, k, :], h_lo[:, k, :],
                                                k == 0, k == KD - 1)
                            mm.then_inc(a_done, 1)

            @block.scalar
            def _(act):
                def round_(L, q, r, landings):
                    a = slice(q * QUARTER, (q + 1) * QUARTER)
                    act.wait_ge(u_in[r], landings)
                    act.wait_ge(a_done, L + 1)
                    act.activation(u_hi[:, r, a], u_raw[:, r, a], ACT.Copy).then_inc(hi_done, 1)

                act.sem_inc(kept, BANK_FREE)
                act.sem_inc(gelu_done, A_FREE)
                for q in range(ROUNDED):
                    round_(q, q % 4, q // 4, 16)
                PER_TILE = P // (8 * BATCH)
                for t in range(TT):
                    if t >= 2:
                        act.wait_ge(stored[t % 2], 16 * PARTS)
                    with act.Fori(0, PER_TILE) as i:
                        for e in range(2):
                            for b in range(4):
                                B = 8 * i + (8 * PER_TILE * t + 4 * e + b)
                                tile = 2 * PER_TILE * t + e + (b + ROUNDED) // 4
                                round_(B + ROUNDED, (b + ROUNDED) % 4, tile % 2, 16 * i + 16 * (tile // 2 + 1))
                                act.wait_ge(used, B + (HOT_FREE + 1))
                                act.activation(dense[:, t % 2, :, bass.ds((8 * i + (4 * e + b)) * BATCH, BATCH)],
                                               ps[:, b, :].rearrange("p (c j) -> p j c", c=BATCH), ACT.Copy).then_inc(kept, 1)
                            s = 2 * i + (2 * PER_TILE * t + e)
                            act.wait_ge(a_done, 4 * s + (U_FREE + 4))
                            act.wait_ge(result_free, s + 1)
                            act.activation(result[:, e, :], ps[:, 4 + e, :], ACT.Gelu).then_inc(gelu_done, 1)

            @block.sync
            def _(sp):
                for t in range(TT):
                    for c in range(PARTS):
                        sp.wait_ge(kept, BANK_FREE + (P // BATCH) * (t + 1) + (c * 3 if t < TT - 1 else 0))
                        a = slice(c * NKEYS // PARTS, (c + 1) * NKEYS // PARTS)
                        sp.dma_start(G_d[:, a, t * P:t * P + P], dense[:, t % 2, a]).then_inc(stored[t % 2], 16)
                sp.wait_ge(stored[0], 16 * 2 * PARTS)
                sp.wait_ge(stored[1], 16 * 2 * PARTS)


def early(nc, ps, xT, y, V_d, G_d, early_d, x_d):
    GT = 4
    NG = EARLY // GT
    with nc.cleanup_on_exit(), ExitStack() as ctx:
        sb = lambda n, s, d=F32: ctx.enter_context(nc.sbuf_tensor("l_" + n, s, d))
        sem = lambda n: nc.alloc_semaphore("l_" + n)
        v_raw, v_hi, v_lo = sb("v_raw", [P, GT, D]), sb("v_hi", [P, 2, D], F32R), sb("v_lo", [P, 2, D], F32R)
        w_hi, w_lo, full = sb("w_hi", [P, 2, TOK], F32R), sb("w_lo", [P, 2, TOK], F32R), sb("full", [P, 2, TOK])
        G, act_in = sb("G", [P, 2, GT, TOK]), sb("act_in", [P, 2, GT, TOK])
        v_in, g_in, e_in = [sem(f"v_in{t}") for t in range(GT)], [sem("g_in0"), sem("g_in1")], [sem("e_in0"), sem("e_in1")]
        v_hi_done, v_lo_done, full_done, w_hi_done, w_done = sem("v_hi_done"), sem("v_lo_done"), sem("full_done"), sem("w_hi_done"), sem("w_done")
        mixed, x_in, y_done = sem("mixed"), sem("x_in"), sem("y_done")

        with nc.Block() as block:
            @block.sync
            def _(sp):
                def group(g, gp, first=False):
                    if not first:
                        sp.wait_ge(full_done, GT * g - GT)
                    sp.dma_start(G[:, gp], G_d[:, bass.ds(GT * g, GT), :]).then_inc(g_in[gp], 16)
                    sp.dma_start(act_in[:, gp], early_d[bass.ds(GT * g, GT)].rearrange("n p c -> p n c")).then_inc(e_in[gp], 16)
                    for t in range(GT):
                        if not first or g > 0:
                            sp.wait_ge(v_lo_done, GT * g + (t - GT + 1))
                        sp.dma_start(v_raw[:, t, :], V_d[:, bass.ds(GT * g + t, 1), :].rearrange("p o n -> p (o n)")).then_inc(v_in[t], 16)

                group(0, 0, True)
                group(1, 1, True)
                sp.dma_start(xT[:], x_d).then_inc(x_in, 16)
                with sp.Fori(1, NG // 2) as i:
                    group(2 * i, 0)
                    group(2 * i + 1, 1)
                sp.wait_ge(x_in, 16)

            @block.scalar
            def _(act):
                def V(g, t, first=False):
                    act.wait_ge(v_in[t], 16 * g + 16)
                    if not first:
                        act.wait_ge(mixed, GT * g + (t - 1))
                    act.activation(v_hi[:, t % 2, :], v_raw[:, t, :], ACT.Copy).then_inc(v_hi_done, 1)

                for t in range(GT):
                    V(0, t, first=t < 2)
                with act.Fori(1, NG) as g:
                    for t in range(GT):
                        V(g, t)
                for m in range(0, KD, 2):
                    act.wait_ge(mixed, EARLY)
                    act.activation(y[:, m, :], ps[:, m, :], ACT.Copy).then_inc(y_done, 1)

            @block.vector
            def _(dve):
                def step(g, gp, t, landings, first=False):
                    n = GT * g + t
                    dve.wait_ge(v_hi_done, n + 1)
                    dve.tensor_tensor(v_lo[:, t % 2, :], v_raw[:, t, :], v_hi[:, t % 2, :].bitcast(F32), ALU.subtract).then_inc(v_lo_done, 1)
                    if t == 0:
                        dve.wait_ge(g_in[gp], landings)
                        dve.wait_ge(e_in[gp], landings)
                    if not first:
                        dve.wait_ge(w_done, n - 1)
                    dve.tensor_tensor(full[:, t % 2, :], act_in[:, gp, t, :], G[:, gp, t, :], ALU.mult).then_inc(full_done, 1)
                    dve.wait_ge(full_done, n + 1)
                    if not first:
                        dve.wait_ge(mixed, n - 1)
                    dve.tensor_copy(w_hi[:, t % 2, :], full[:, t % 2, :]).then_inc(w_hi_done, 1)
                    dve.wait_ge(w_hi_done, n + 1)
                    dve.tensor_tensor(w_lo[:, t % 2, :], full[:, t % 2, :], w_hi[:, t % 2, :].bitcast(F32), ALU.subtract).then_inc(w_done, 1)

                for g in range(2):
                    for t in range(GT):
                        step(g, g, t, 16, first=g == 0 and t < 2)
                with dve.Fori(1, NG // 2) as i:
                    for gp in range(2):
                        for t in range(GT):
                            step(2 * i + gp, gp, t, 16 * i + 16)
                for m in range(1, KD, 2):
                    dve.wait_ge(mixed, EARLY)
                    dve.tensor_copy(y[:, m, :], ps[:, m, :]).then_inc(y_done, 1)

            @block.tensor
            def _(pe):
                def tile(g, t, first=False, last=False):
                    n = GT * g + t
                    pe.wait_ge(v_lo_done, n + 1)
                    pe.wait_ge(w_done, n + 1)
                    for m in range(KD):
                        a = slice(m * P, m * P + P)
                        mm = three_pass(pe, ps[:, m, :], v_hi[:, t % 2, a], v_lo[:, t % 2, a], w_hi[:, t % 2, :], w_lo[:, t % 2, :],
                                        first, last)
                    mm.then_inc(mixed, 1)

                for t in range(GT):
                    tile(0, t, first=t == 0)
                with pe.Fori(1, NG - 1) as g:
                    for t in range(GT):
                        tile(g, t)
                for t in range(GT):
                    tile(NG - 1, t, last=t == GT - 1)


def experts(nc, ps, xT, y, h_hi, h_lo, ones, col, modc, U_d, V_d, G_d):
    GT = 4
    TILES = NKEYS - EARLY
    NG = TILES // GT
    with nc.cleanup_on_exit(), ExitStack() as ctx:
        sb = lambda n, s, d=F32: ctx.enter_context(nc.sbuf_tensor("e_" + n, s, d))
        sem = lambda n: nc.alloc_semaphore("e_" + n)
        u_raw, u_hi, u_lo = sb("u_raw", [P, GT, SLOT]), sb("u_hi", [P, 2, SLOT], F32R), sb("u_lo", [P, 2, SLOT], F32R)
        v_raw, v_hi, v_lo = sb("v_raw", [P, GT, D]), sb("v_hi", [P, GT, D], F32R), sb("v_lo", [P, GT, D], F32R)
        w_hi, w_lo = sb("w_hi", [P, 2, GT, TOK], F32R), sb("w_lo", [P, 2, GT, TOK], F32R)
        G = sb("G", [P, 2, GT, TOK])
        gelu, w_full = sb("gelu", [P, 2, TOK]), sb("w_full", [P, 2, TOK])
        u_in, v_in = [sem(f"u_in{i}") for i in range(GT)], [sem(f"v_in{i}") for i in range(GT)]
        g_in = [sem("g_in0"), sem("g_in1")]
        u_hi_done, u_lo_done, v_hi_done, v_lo_done = sem("u_hi_done"), sem("u_lo_done"), sem("v_hi_done"), sem("v_lo_done")
        a_done, gelu_done, full_done, w_hi_done, w_done = sem("a_done"), sem("gelu_done"), sem("full_done"), sem("w_hi_done"), sem("w_done")
        part_done, added = sem("part_done"), sem("added")
        A_FREE, G_FREE, ADD_FREE = 2, 2, 4
        fin_added, fin_done = sem("fin_added"), sem("fin_done")
        norms = Norms(ctx, nc, "e_norms", ps[:, 5, :], w_full, gelu)

        with nc.Block() as block:
            @block.sync
            def _(sp):
                def group(g, gp, u=True, v=True, reuse_u=True, reuse_v=True, reuse_g=True):
                    if u:
                        if reuse_g:
                            sp.wait_ge(full_done, GT * g + (G_FREE - GT))
                        sp.dma_start(G[:, gp], G_d[:, bass.ds(GT * g + EARLY, GT), :]).then_inc(g_in[gp], 16)
                    for t in range(GT):
                        if u:
                            if reuse_u:
                                sp.wait_ge(u_lo_done, GT * g + (t - GT + 1))
                            sp.dma_start(u_raw[:, t, :], U_d[bass.ds(GT * g + (t + EARLY), 1)].rearrange("o p n -> p (o n)")).then_inc(u_in[t], 16)
                        if v:
                            if reuse_v:
                                sp.wait_ge(v_lo_done, GT * g + (t - 2 * GT + 1))
                            sp.dma_start(v_raw[:, t, :], V_d[:, bass.ds(GT * g + (t - GT + EARLY), 1), :].rearrange("p o n -> p (o n)")).then_inc(v_in[t], 16)

                group(0, 0, v=False, reuse_u=False, reuse_g=False)
                group(1, 1, reuse_v=False, reuse_g=False)
                with sp.Fori(1, NG // 2) as i:
                    group(2 * i, 0)
                    group(2 * i + 1, 1)
                group(NG, 0, u=False)

            @block.tensor
            def _(pe):
                def A(g, t):
                    n = GT * g + t
                    pe.wait_ge(u_lo_done, n + 1)
                    pe.wait_ge(gelu_done, n + 1)
                    for k in range(KD):
                        s = slice(k * P, k * P + P)
                        mm = three_pass(pe, ps[:, 6 + t % 2, :], u_hi[:, t % 2, s], u_lo[:, t % 2, s], h_hi[:, k, :],
                                        h_lo[:, k, :], k == 0, k == KD - 1)
                    mm.then_inc(a_done, 1)

                def Y(g, gp):
                    pe.wait_ge(w_done, GT * g + GT)
                    pe.wait_ge(v_lo_done, GT * g + GT)
                    for m in range(KD):
                        pe.wait_ge(added, KD * g + m + 1)
                        for t in range(GT):
                            s = slice(m * P, m * P + P)
                            mm = three_pass(pe, ps[:, m % 4, :], v_hi[:, t, s], v_lo[:, t, s], w_hi[:, gp, t, :],
                                            w_lo[:, gp, t, :], t == 0, t == GT - 1)
                        mm.then_inc(part_done, 1)

                def group(g, gp):
                    for t in range(GT):
                        A(g, t)
                    Y(g - 1, 1 - gp)

                for t in range(GT):
                    A(0, t)
                with pe.Fori(0, NG // 2 - 1) as i:
                    group(2 * i + 1, 1)
                    group(2 * i + 2, 0)
                group(NG - 1, 1)
                Y(NG - 1, 1)
                norms.sums(pe, ones[:], 0, 0, KD)

            @block.scalar
            def _(act):
                def U(g, t, first=False):
                    n = GT * g + t
                    act.wait_ge(u_in[t], 16 * g + 16)
                    if not first:
                        act.wait_ge(a_done, n - 1)
                    act.activation(u_hi[:, t % 2, :], u_raw[:, t, :], ACT.Copy).then_inc(u_hi_done, 1)

                def V(g, t, first=False):
                    act.wait_ge(v_in[t], 16 * g + 16)
                    if not first:
                        act.wait_ge(part_done, KD * g)
                    act.activation(v_hi[:, t, :], v_raw[:, t, :], ACT.Copy).then_inc(v_hi_done, 1)

                def step(g, t, v=True, v_first=False, ahead=True):
                    if v:
                        V(g - 1, t, v_first)
                    n = GT * g + t
                    act.wait_ge(a_done, n + 1)
                    act.wait_ge(full_done, n + 1)
                    act.activation(gelu[:, t % 2, :], ps[:, 6 + t % 2, :], ACT.Gelu).then_inc(gelu_done, 1)
                    if ahead:
                        U(g + (t + 2) // GT, (t + 2) % GT)

                act.sem_inc(gelu_done, A_FREE)
                U(0, 0, True)
                U(0, 1, True)
                for t in range(GT):
                    step(0, t, v=False)
                for t in range(GT):
                    step(1, t, v_first=True)
                with act.Fori(1, NG // 2 - 1) as i:
                    for gp in range(2):
                        for t in range(GT):
                            step(2 * i + gp, t)
                for g in (NG - 2, NG - 1):
                    for t in range(GT):
                        step(g, t, ahead=GT * g + t + 2 < TILES)
                for t in range(GT):
                    V(NG - 1, t)
                act.wait_ge(fin_added, KD)
                norms.squares(act, 0, [xT[:, k, :] for k in range(KD)])
                norms.root(act, 0)

            @block.vector
            def _(dve):
                def U(g, t):
                    n = GT * g + t
                    dve.wait_ge(u_hi_done, n + 1)
                    dve.tensor_tensor(u_lo[:, t % 2, :], u_raw[:, t, :], u_hi[:, t % 2, :].bitcast(F32), ALU.subtract).then_inc(u_lo_done, 1)

                def V(g, t):
                    dve.wait_ge(v_hi_done, GT * g + t + 1)
                    dve.tensor_tensor(v_lo[:, t, :], v_raw[:, t, :], v_hi[:, t, :].bitcast(F32), ALU.subtract).then_inc(v_lo_done, 1)

                def W(g, gp, t):
                    n = GT * g + t
                    if t == 0:
                        dve.wait_ge(g_in[gp], 8 * (g - gp) + 16)
                    dve.wait_ge(gelu_done, n + (A_FREE + 1))
                    dve.tensor_tensor(w_full[:, t % 2, :], gelu[:, t % 2, :], G[:, gp, t, :], ALU.mult).then_inc(full_done, 1)
                    dve.wait_ge(full_done, n + (G_FREE + 1))
                    dve.tensor_copy(w_hi[:, gp, t, :], w_full[:, t % 2, :]).then_inc(w_hi_done, 1)
                    dve.wait_ge(w_hi_done, n + 1)
                    dve.tensor_tensor(w_lo[:, gp, t, :], w_full[:, t % 2, :], w_hi[:, gp, t, :].bitcast(F32), ALU.subtract).then_inc(w_done, 1)

                def Y(g):
                    for m in range(KD):
                        dve.wait_ge(part_done, KD * g + m + 1)
                        dve.tensor_tensor(y[:, m, :], y[:, m, :], ps[:, m % 4, :], ALU.add).then_inc(added, 1)

                def step(g, gp, t, v=True, ahead=True):
                    if v:
                        V(g - 1, t)
                    W(g, gp, t)
                    if ahead:
                        U(g + (t + 2) // GT, (t + 2) % GT)

                dve.sem_inc(added, ADD_FREE)
                dve.sem_inc(full_done, G_FREE)
                U(0, 0)
                U(0, 1)
                for t in range(GT):
                    step(0, 0, t, v=False)
                for t in range(GT):
                    step(1, 1, t)
                Y(0)
                with dve.Fori(1, NG // 2 - 1) as i:
                    for gp in range(2):
                        for t in range(GT):
                            step(2 * i + gp, gp, t)
                        Y(2 * i + gp - 1)
                for gp in range(2):
                    g = NG - 2 + gp
                    for t in range(GT):
                        step(g, gp, t, ahead=GT * g + t + 2 < TILES)
                    Y(g - 1)
                for t in range(GT):
                    V(NG - 1, t)
                Y(NG - 1)
                dve.wait_ge(added, ADD_FREE + KD * NG)
                for m in range(KD):
                    dve.scalar_tensor_tensor(out=xT[:, m, :], in0=y[:, m, :], scalar=modc(5, m), in1=xT[:, m, :],
                                             op0=ALU.mult, op1=ALU.add).then_inc(fin_added, 1)
                norms.inverse(dve, 0, KD, D)
                dve.wait_ge(norms.rstd_ready, 1)
                for m in range(KD):
                    dve.scalar_tensor_tensor(out=xT[:, m, :], in0=xT[:, m, :], scalar=col("final_norm", m),
                                             in1=norms.rstd[:, 0, :], op0=ALU.mult, op1=ALU.mult).then_inc(fin_done, 1)


def mixer2(nc, ps, xT, ident, ones, col, tabs_d, w_in2_d, pool_w_d, w_out2_d):
    K, Q0, V, U0, POOL, OUT = 0, 1, 5, 6, 10, 14
    items = [("split", w_in2_d[m], SLOT) for m in range(10)] + [("split", pool_w_d, TOK)]
    items += [("split", w_out2_d[m], SLOT) for m in range(KD)]
    last_block = list(range(10)) + [POOL + 3] + [OUT + m for m in range(KD)]
    released = {j: s for s, j in enumerate(last_block)}
    PAD = max(POOL_WINDOWS) // 2
    LONG = TOK + 2 * PAD
    with nc.cleanup_on_exit(), ExitStack() as ctx:
        sb = lambda n, s, d=F32: ctx.enter_context(nc.sbuf_tensor("b_" + n, s, d))
        sem = lambda n: nc.alloc_semaphore("b_" + n)
        stream = Stream(ctx, nc, "b_w", 4, 2, items, last_block)
        projected = stream.projected
        norms = Norms(ctx, nc, "b_norms", ps[:, 7, :])
        normed = Normed(ctx, nc, "b_normed")
        rotation = Rotation(ctx, nc, "b_rot", [ps[:, 2, :], ps[:, 3, :]])
        turn = Turn(ctx, nc, "b_turn", [ps[:, 2, :], ps[:, 3, :]], ident[:])
        in_hi, in_lo = sb("in_hi", [P, KD, TOK], F32R), sb("in_lo", [P, KD, TOK], F32R)
        tables = ["pair_ax", "ones_heads", "C_ax", "S_ax", "inv_cnt"]
        tab = {n: sb(n, [P, TABS[n][1]]) for n in tables}
        raw_qk = sb("raw_qk", [P, 2, TOK])
        k_rot, q_rot, v = sb("k_rot", [P, TOK]), sb("q_rot", [P, 4, TOK]), sb("v", [P, TT, P])
        o_tok = sb("o_tok", [P, TT, TOK])
        u = sb("u", [P, 4, LONG])
        win = sb("win", [P, 2, LONG])
        pooled = sb("pooled", [P, 4, TOK])
        pool_hi, pool_lo = sb("pool_hi", [P, 4, TOK], F32R), sb("pool_lo", [P, 4, TOK], F32R)
        loaded, kept, head_normed, padded, pool_step = sem("loaded"), sem("kept"), sem("head_normed"), sem("padded"), sem("pool_step")
        pool_done, pool_hi_done, pool_lo_done = sem("pool_done"), sem("pool_hi_done"), sem("pool_lo_done")
        mix_full, mix_hi, mix_lo, added = sem("mix_full"), sem("mix_hi"), sem("mix_lo"), sem("added")
        units = []
        for h, t in SWA_UNITS:
            g = h // 4
            rows = slice(g * HD, g * HD + HD)
            units.append((q_rot[rows, h % 4, t * P:t * P + P], k_rot[rows, :], lambda key, g=g: v[:, key, g * HD:g * HD + HD],
                          list(range(TT)), SCALE, None))
        buffers = ([normed.x[:, 0, :], normed.x[:, 1, :], rotation.t[:, 0, 0, :]],
                   [normed.full[:, 0, :], normed.full[:, 1, :], rotation.t[:, 0, 1, :]], [])
        outs = [o_tok[:, t, :].rearrange("p (h d) -> p h d", h=NH) for t in range(TT)]
        attention = Attention(ctx, nc, "b_att", ps, units, ident[:], *buffers, outs, [None] * TT)
        NLOADS = len(tables)
        mix = rotation.x

        with nc.Block() as block:
            @block.sync
            def _(sp):
                stream.loads(sp, 0, 4)
                for name, dst in tab.items():
                    o, w = TABS[name]
                    sp.dma_start(dst[:], tabs_d[:, o:o + w]).then_inc(loaded, 16)
                stream.loads(sp, 4)

            @block.tensor
            def _(pe):
                norms.sums(pe, ones[:], 0, 0, KD)
                pe.wait_ge(loaded, 16 * NLOADS)

                def heads(n):
                    if n < 5:
                        norms.sums(pe, tab["ones_heads"][:], n + 1, KD + n, 1)
                    if n:
                        rotation.pe(pe, n - 1, tab["pair_ax"][:], head_normed, n)

                for j in range(10):
                    if j >= 2:
                        pe.wait_ge(kept, j - 1)
                    if j == V:
                        pe.wait_ge(stream.lo_ready, j + 1)
                        for t in range(TT):
                            for k in range(KD):
                                w_hi, w_lo = stream.weights(j, k * P, k * P + P)
                                mm = three_pass(pe, ps[:, j % 2, t * P:t * P + P], in_hi[:, k, t * P:t * P + P],
                                                in_lo[:, k, t * P:t * P + P], w_hi, w_lo, k == 0, k == KD - 1)
                        mm.then_inc(projected, 1)
                    else:
                        dense_block(pe, stream, j, ps[:, j % 2, :], in_hi, in_lo, x_ready=normed.lo_done if j == 0 else None).then_inc(projected, 1)
                    if 1 <= j <= 6:
                        heads(j - 1)
                pe.wait_ge(kept, POOL)
                pe.wait_ge(rotation.done, 5)
                attention.pe(pe)
                pe.wait_ge(stream.lo_ready, 11)
                for g in range(4):
                    j = POOL + g
                    pe.wait_ge(pool_lo_done, g + 1)
                    if g >= 2:
                        pe.wait_ge(mix_full, g - 1)
                    else:
                        pe.wait_ge(attention.exp_done, len(units))
                    w_hi, w_lo = stream.weights(10, g * P, g * P + P)
                    three_pass(pe, ps[:, j % 2, :], w_hi, w_lo, pool_hi[:, g, :], pool_lo[:, g, :], True, True).then_inc(projected, 1)
                pe.wait_ge(attention.out_done, TT)
                for n in range(4):
                    turn.pe(pe, n, lambda t: o_tok[:, t, n * P:n * P + P])
                pe.wait_ge(turn.lo_done, 4)
                pe.wait_ge(mix_lo, 4)
                for m in range(KD):
                    if m >= 2:
                        pe.wait_ge(added, m - 1)
                    dense_block(pe, stream, 11 + m, ps[:, m % 2, :], in_hi, in_lo).then_inc(projected, 1)

            @block.gpsimd
            def _(pool):
                pool.memset(u[:], 0.0).then_inc(padded, 1)
                steps = 0
                for g, w in enumerate(POOL_WINDOWS):
                    pool.wait_ge(kept, U0 + g + 1)
                    src, length, shift = u[:, g, :], LONG, 1
                    for s in range(g + 1):
                        length -= shift
                        dst = win[:, s % 2, 0:length]
                        pool.tensor_tensor(dst, src[:, 0:length], src[:, shift:shift + length], ALU.add).then_inc(pool_step, 1)
                        steps += 1
                        pool.wait_ge(pool_step, steps)
                        src, shift = win[:, s % 2, :], 2 * shift
                    first = PAD - w // 2
                    o = pooled[:, g, :]
                    pool.tensor_tensor(o, src[:, first:first + TOK], tab["inv_cnt"][:, g * TOK:(g + 1) * TOK], ALU.mult).then_inc(pool_step, 1)
                    steps += 1
                    pool.wait_ge(pool_step, steps)
                    pool.tensor_tensor(o, o, u[:, g, PAD:PAD + TOK], ALU.subtract).then_inc(pool_done, 1)

            @block.scalar
            def _(act):
                norms.squares(act, 0, [xT[:, k, :] for k in range(KD)])
                stream.split_hi(act, 0)
                stream.split_hi(act, 1)
                norms.root(act, 0)
                normed.act(act, 0, in_hi, KD)
                act.wait_ge(padded, 1)
                for j in range(10):
                    act.wait_ge(projected, j + 1)
                    src = ps[:, j % 2, :]
                    if j < V:
                        if j >= 2:
                            act.wait_ge(head_normed, j - 1)
                        act.activation(raw_qk[:, j % 2, :], src, ACT.Copy).then_inc(kept, 1)
                        stream.split_hi(act, j + stream.Q)
                        act.wait_ge(kept, j + 1)
                        norms.squares(act, KD + j, [raw_qk[:, j % 2, :]])
                        if j:
                            norms.root(act, j)
                    elif j == V:
                        act.activation(v[:], src.rearrange("p (t c) -> p t c", t=TT), ACT.Copy).then_inc(kept, 1)
                        stream.split_hi(act, j + stream.Q)
                        norms.root(act, V)
                    else:
                        act.activation(u[:, j - U0, PAD:PAD + TOK], src, ACT.Copy).then_inc(kept, 1)
                        stream.split_hi(act, j + stream.Q)
                attention.act(act)
                for g in range(4):
                    act.wait_ge(pool_done, g + 1)
                    act.activation(pool_hi[:, g, :], pooled[:, g, :], ACT.Copy).then_inc(pool_hi_done, 1)
                for g in range(4):
                    act.wait_ge(mix_full, g + 1)
                    act.activation(in_hi[:, 4 + g, :], mix[:, g % 2, :], ACT.Copy).then_inc(mix_hi, 1)
                stream.split_hi(act, 12)
                for n in range(4):
                    act.wait_ge(turn.turned, n + 1)
                    act.activation(in_hi[:, n, :], turn.banks[n % 2], ACT.Copy).then_inc(turn.hi_done, 1)
                for m in range(KD):
                    stream.split_hi(act, 13 + m)

            @block.vector
            def _(dve):
                norms.inverse(dve, 0, KD, D)
                stream.split_lo(dve, 0)
                stream.split_lo(dve, 1)
                dve.wait_ge(norms.rstd_ready, 1)
                normed.dve(dve, 0, lambda k: xT[:, k, :], norms.rstd[:, 0, :], lambda k: col("norm1_g_2", k), None,
                           in_hi, in_lo, KD)
                dve.wait_ge(loaded, 16 * NLOADS)

                def rotate(n):
                    out = k_rot[:] if n == 0 else q_rot[:, n - 1, :]
                    rotation.dve(dve, n, out, tab["C_ax"][:], tab["S_ax"][:], head_normed, n + 1)

                for j in range(10):
                    stream.split_lo(dve, j + stream.Q)
                    if 1 <= j <= V:
                        n = j - 1
                        norms.inverse(dve, n + 1, KD + n + 1, HD)
                        dve.wait_ge(norms.rstd_ready, n + 2)
                        rotation.x_free(dve, n)
                        dve.scalar_tensor_tensor(out=rotation.x[:, n % 2, :], in0=raw_qk[:, n % 2, :],
                                                 scalar=col("k_gain" if n == 0 else "q_gain"), in1=norms.rstd[:, (n + 1) % 2, :],
                                                 op0=ALU.mult, op1=ALU.mult).then_inc(head_normed, 1)
                        if n:
                            rotate(n - 1)
                    if j == U0:
                        rotate(4)
                attention.dve(dve)
                for g in range(4):
                    dve.wait_ge(pool_hi_done, g + 1)
                    dve.tensor_tensor(pool_lo[:, g, :], pooled[:, g, :], pool_hi[:, g, :].bitcast(F32), ALU.subtract).then_inc(pool_lo_done, 1)

                def mix_rest(g):
                    dve.wait_ge(mix_hi, g + 1)
                    dve.tensor_tensor(in_lo[:, 4 + g, :], mix[:, g % 2, :], in_hi[:, 4 + g, :].bitcast(F32), ALU.subtract).then_inc(mix_lo, 1)

                for g in range(4):
                    dve.wait_ge(projected, POOL + g + 1)
                    if g >= 2:
                        dve.wait_ge(mix_lo, g - 1)
                    dve.tensor_scalar(mix[:, g % 2, :], ps[:, g % 2, :], col("pool_b", g), col("pool_scale", g), ALU.add,
                                      ALU.mult).then_inc(mix_full, 1)
                    if g:
                        mix_rest(g - 1)
                mix_rest(3)
                stream.split_lo(dve, 12)
                for n in range(4):
                    dve.wait_ge(turn.hi_done, n + 1)
                    dve.tensor_tensor(in_lo[:, n, :], turn.banks[n % 2], in_hi[:, n, :].bitcast(F32), ALU.subtract).then_inc(turn.lo_done, 1)
                for m in range(KD):
                    stream.split_lo(dve, 13 + m)
                    dve.wait_ge(projected, OUT + m + 1)
                    dve.tensor_tensor(xT[:, m, :], ps[:, m % 2, :], xT[:, m, :], ALU.add).then_inc(added, 1)


def swiglu(nc, ps, xT, ones, col, w_gu_d, w_down_d, out_d):
    RAW = 4
    PARTS = 3
    PER_PART = [KD, KD, FB - 2 * KD]
    STEPS = FB // 2
    with nc.cleanup_on_exit(), ExitStack() as ctx:
        sb = lambda n, s, d=F32: ctx.enter_context(nc.sbuf_tensor("f_" + n, s, d))
        sem = lambda n: nc.alloc_semaphore("f_" + n)
        raw, hi, lo = sb("raw", [P, RAW, SLOT]), sb("hi", [P, 2, SLOT], F32R), sb("lo", [P, 2, SLOT], F32R)
        norms = Norms(ctx, nc, "f_norms", ps[:, 7, :])
        normed = Normed(ctx, nc, "f_normed")
        in_hi, in_lo = sb("in_hi", [P, KD, TOK], F32R), sb("in_lo", [P, KD, TOK], F32R)
        act_hi, act_lo = sb("act_hi", [P, FB, TOK], F32R), sb("act_lo", [P, FB, TOK], F32R)
        silu, full = norms.sq, normed.full
        landed = [sem(f"landed{i}") for i in range(RAW)]
        hi_ready, lo_ready, projected = sem("hi_ready"), sem("lo_ready"), sem("projected")
        silu_done, full_done, act_hi_done, act_lo_done = sem("silu_done"), sem("full_done"), sem("act_hi_done"), sem("act_lo_done")
        summed, added, stored = sem("summed"), sem("added"), sem("stored")
        down = [(m, c) for m in range(KD) for c in range(PARTS)]
        GU = 2 * FB
        FREE = 2

        with nc.Block() as block:
            @block.sync
            def _(sp):
                for n in range(RAW):
                    sp.dma_start(raw[:, n, :], w_gu_d[n]).then_inc(landed[n], 16)
                with sp.Fori(1, STEPS) as i:
                    for r in range(RAW):
                        sp.wait_ge(lo_ready, RAW * i + (r - RAW + 1))
                        sp.dma_start(raw[:, r, :], w_gu_d[bass.ds(RAW * i + r, 1)].rearrange("o p n -> p (o n)")).then_inc(landed[r], 16)
                for d, (m, c) in enumerate(down):
                    n = GU + d
                    sp.wait_ge(lo_ready, n - RAW + 1)
                    w = PER_PART[c] * P
                    sp.dma_start(raw[:, n % RAW, 0:w], w_down_d[m, c, :, 0:w]).then_inc(landed[n % RAW], 16)
                for m in range(KD):
                    sp.wait_ge(added, m + 1)
                    sp.dma_start(out_d[:, m, :], xT[:, m, :]).then_inc(stored, 16)
                sp.wait_ge(stored, 16 * KD)

            @block.tensor
            def _(pe):
                norms.sums(pe, ones[:], 0, 0, KD)
                with pe.Fori(0, STEPS) as i:
                    for r in range(RAW):
                        pe.wait_ge(lo_ready, RAW * i + (r + 1))
                        if r % 2 == 0:
                            pe.wait_ge(full_done, 2 * i + (r // 2 + 1))
                        for k in range(KD):
                            if r == 0:
                                pe.wait_ge(normed.lo_done, k + 1)
                            s = slice(k * P, k * P + P)
                            mm = three_pass(pe, ps[:, r, :], hi[:, r % 2, s], lo[:, r % 2, s], in_hi[:, k, :], in_lo[:, k, :],
                                            k == 0, k == KD - 1)
                        mm.then_inc(projected, 1)
                pe.wait_ge(act_lo_done, FB)
                for d, (m, c) in enumerate(down):
                    n = GU + d
                    pe.wait_ge(lo_ready, n + 1)
                    if c == 0 and m >= 2:
                        pe.wait_ge(added, m - 1)
                    for k in range(PER_PART[c]):
                        s, f = slice(k * P, k * P + P), c * KD + k
                        mm = three_pass(pe, ps[:, 4 + m % 2, :], hi[:, n % 2, s], lo[:, n % 2, s], act_hi[:, f, :], act_lo[:, f, :],
                                        f == 0, f == FB - 1)
                    mm.then_inc(projected, 1)

            @block.scalar
            def _(act):
                def split(n, r, landings, free=True, w=SLOT):
                    act.wait_ge(landed[r], landings)
                    if free:
                        act.wait_ge(projected, n - 1)
                    act.activation(hi[:, r % 2, 0:w], raw[:, r, 0:w], ACT.Copy).then_inc(hi_ready, 1)

                def feature(i, f, more=(True, True)):
                    act.wait_ge(projected, 4 * i + (2 * f + 1))
                    act.wait_ge(full_done, 2 * i + (f + 1))
                    act.activation(silu[:, f, :], ps[:, 2 * f, :], ACT.Silu).then_inc(silu_done, 1)
                    if more[0]:
                        r = (2 * f + 2) % RAW
                        split(4 * i + (2 * f + 2), r, 16 * i + 16 * (1 + (2 * f + 2) // RAW))
                    act.wait_ge(full_done, 2 * i + (f + 1 + FREE))
                    act.activation(act_hi[:, bass.ds(2 * i + f, 1), :].rearrange("p o n -> p (o n)"), full[:, f, :], ACT.Copy).then_inc(act_hi_done, 1)
                    if more[1]:
                        r = (2 * f + 3) % RAW
                        split(4 * i + (2 * f + 3), r, 16 * i + 16 * (1 + (2 * f + 3) // RAW))

                norms.squares(act, 0, [xT[:, k, :] for k in range(KD)])
                split(0, 0, 16, False)
                split(1, 1, 16, False)
                norms.root(act, 0)
                normed.act(act, 0, in_hi, KD)
                with act.Fori(0, STEPS - 1) as i:
                    feature(i, 0)
                    feature(i, 1)
                feature(STEPS - 1, 0)
                feature(STEPS - 1, 1)
                for d in range(2, len(down)):
                    n = GU + d
                    split(n, n % RAW, 16 * (n // RAW + 1), w=PER_PART[d % PARTS] * P)

            @block.vector
            def _(dve):
                def split(n, r, w=SLOT):
                    dve.wait_ge(hi_ready, n + 1)
                    dve.tensor_tensor(lo[:, r % 2, 0:w], raw[:, r, 0:w], hi[:, r % 2, 0:w].bitcast(F32), ALU.subtract).then_inc(lo_ready, 1)

                def feature(i, f):
                    split(4 * i + (2 * f + 2), (2 * f + 2) % RAW)
                    dve.wait_ge(silu_done, 2 * i + (f + 1))
                    dve.wait_ge(projected, 4 * i + (2 * f + 2))
                    dve.tensor_tensor(full[:, f, :], silu[:, f, :], ps[:, 2 * f + 1, :], ALU.mult).then_inc(full_done, 1)
                    split(4 * i + (2 * f + 3), (2 * f + 3) % RAW)
                    dve.wait_ge(act_hi_done, 2 * i + (f + 1))
                    dve.tensor_tensor(act_lo[:, bass.ds(2 * i + f, 1), :].rearrange("p o n -> p (o n)"), full[:, f, :],
                                      act_hi[:, bass.ds(2 * i + f, 1), :].rearrange("p o n -> p (o n)").bitcast(F32), ALU.subtract).then_inc(act_lo_done, 1)

                dve.sem_inc(full_done, FREE)
                norms.inverse(dve, 0, KD, D)
                split(0, 0)
                split(1, 1)
                dve.wait_ge(norms.rstd_ready, 1)
                normed.dve(dve, 0, lambda k: xT[:, k, :], norms.rstd[:, 0, :], lambda k: col("norm2_g_2", k), None,
                           in_hi, in_lo, KD)
                with dve.Fori(0, STEPS) as i:
                    feature(i, 0)
                    feature(i, 1)
                for d, (m, c) in enumerate(down):
                    if d + 2 < len(down):
                        split(GU + d + 2, (GU + d + 2) % RAW, PER_PART[(d + 2) % PARTS] * P)
                    if c == PARTS - 1:
                        dve.wait_ge(projected, GU + d + 1)
                        dve.tensor_tensor(xT[:, m, :], ps[:, 4 + m % 2, :], xT[:, m, :], ALU.add).then_inc(added, 1)


def rotation_tables(dim, pos, rows):
    inv = (np.float32(1.0) / np.power(np.float32(THETA), np.arange(0, dim, 2, dtype=np.float32) / np.float32(dim))).astype(np.float32)
    ang = (pos.astype(np.float32)[None, :] * inv[:, None]).astype(np.float64)
    return np.concatenate([np.cos(ang)] * 2), np.concatenate([-np.sin(ang), np.sin(ang)])


def shape_tables():
    t = np.zeros((P, NTABS), np.float32)

    def put(name, a, rows=slice(0, P)):
        o, w = TABS[name]
        t[rows, o:o + w] = a

    def pairing(dim, rows):
        m = np.zeros((P, P), np.float32)
        for r in rows:
            for i in range(dim):
                m[r + (i + dim // 2) % dim, r + i] = 1.0
        return m

    pos = np.arange(TOK)
    put("ident", np.eye(P))
    put("ones", 1.0)
    put("ones_heads", np.kron(np.eye(2), np.ones((HD, HD))))
    put("pair_swa", pairing(HD, (0, HD)))
    put("pair_mla", pairing(ROPE_D, (HD,)))
    put("pair_ax", pairing(HD // 2, range(0, P, HD // 2)))
    q, k = np.arange(P)[:, None], np.arange(3 * P)[None, :] - P
    put("mask", np.where(np.abs(k - q) <= WINDOW, 0.0, NEG))
    C, S = rotation_tables(HD, pos, None)
    put("C_swa", np.tile(C, (2, 1)))
    put("S_swa", np.tile(S, (2, 1)))
    C, S = rotation_tables(ROPE_D, pos, None)
    put("C_mla", 1.0, slice(0, HD))
    put("C_mla", C, slice(HD, MLA_QK))
    put("S_mla", S, slice(HD, MLA_QK))
    Cr, Sr = rotation_tables(HD // 2, pos // 64, None)
    Cc, Sc = rotation_tables(HD // 2, pos % 64, None)
    put("C_ax", np.concatenate([Cr, Cc] * 2))
    put("S_ax", np.concatenate([Sr, Sc] * 2))
    cnt = [np.minimum(pos - w // 2 + w, TOK) - np.maximum(pos - w // 2, 0) for w in POOL_WINDOWS]
    put("inv_cnt", np.concatenate([1.0 / c for c in cnt])[None, :])
    return t


def by_feature(v):
    return np.asarray(v).reshape(-1, P).T


def blocks_of(w):
    K, M = w.shape
    return np.ascontiguousarray(w.reshape(K // P, P, M // P, P).transpose(2, 1, 0, 3).reshape(M // P, P, K))


def layouts(i):
    a = {k: np.asarray(v) for k, v in i.items()}
    f = np.float32
    x = a["x"][0].T.reshape(KD, P, TOK).transpose(1, 0, 2)
    cols = np.zeros((P, NCOLS), f)
    for name, v in (("b_ada", a["b_ada"][0]), ("mla_q_norm", a["mla_q_norm"][0]), ("mla_kv_norm", a["mla_kv_norm"][0]),
                    ("out_norm", np.concatenate([a["out_norm_swa"][0], a["out_norm_mla"][0]])),
                    ("final_norm", a["final_norm"]), ("norm1_g_2", a["norm1_g_2"][0]),
                    ("q_gain", np.tile(a["q_norm_g_2"][0], 2)), ("k_gain", np.tile(a["k_norm_g_2"][0], 2)),
                    ("pool_b", a["pool_b_2"][0].reshape(-1)), ("pool_scale", a["pool_scale_2"][0]),
                    ("norm2_g_2", a["norm2_g_2"][0]), ("c", a["c"][0])):
        v = by_feature(v)
        cols[:, COLS[name]:COLS[name] + v.shape[1]] = v
    w = a["w_in"][0]
    q, k, v, ql, kvl, kr = np.split(w, np.cumsum([512, 128, 128, 256, 128]), axis=1)
    q = q.reshape(D, 2, 4, HD).transpose(0, 2, 1, 3).reshape(D, 512)
    kr = np.concatenate([np.zeros((D, HD), f), kr, np.zeros((D, P - MLA_QK), f)], axis=1)
    w_in = blocks_of(np.concatenate([ql, kvl, kr, k, q, v], axis=1))
    qu = a["w_mla_q_up"][0].reshape(2, P, NH, MLA_QK).transpose(1, 2, 0, 3)
    qup = np.zeros((P, NH, 2, P), f)
    qup[..., :MLA_QK] = qu
    qup = qup.reshape(P, 2, SLOT).transpose(1, 0, 2)
    kv = a["w_mla_kv_up"][0].reshape(P, NH, 2, HD)
    kv = np.concatenate([kv[:, :, 0].reshape(P, -1), kv[:, :, 1].reshape(P, -1)], axis=1)
    w2 = a["w_in_2"][0]
    q2, k2, v2, u2 = np.split(w2, np.cumsum([512, 128, 128]), axis=1)
    q2 = q2.reshape(D, 2, 4, HD).transpose(0, 2, 1, 3).reshape(D, 512)
    g, u = blocks_of(a["w_gate_2"][0]), blocks_of(a["w_up_2"][0])
    down = np.zeros((KD, P, 3 * KD * P), f)
    down[:, :, :FF] = blocks_of(a["w_down_2"][0])
    U = a["peer_expert_u"][0].reshape(P, NKEYS, KD, P).transpose(1, 3, 2, 0).reshape(NKEYS, P, SLOT)
    return {
        "xT": x, "cols": cols, "sink": np.tile(a["swa_sink"][0][None, :], (P, 1)), "tabs": shape_tables(),
        "w_ada": blocks_of(a["w_ada"][0]), "w_in": w_in, "w_q_up": qup, "w_kv_up": kv, "w_out": blocks_of(a["w_out"][0]),
        "w_query": blocks_of(a["w_peer_query"][0]),
        "keys": a["peer_sub_keys"][0].reshape(NPART, NKEYS, P).transpose(2, 0, 1),
        "U": U, "V": a["peer_expert_v"][0].reshape(P, NKEYS, D),
        "w_in2": blocks_of(np.concatenate([k2, q2, v2, u2], axis=1)),
        "pool_w": a["pool_w_2"][0].transpose(1, 0, 2).reshape(P, TOK), "w_out2": blocks_of(a["w_out_2"][0]),
        "w_gu": np.stack([g, u], axis=1).reshape(2 * FB, P, SLOT), "w_down": down.reshape(KD, P, 3, SLOT).transpose(0, 2, 1, 3),
    }


def kernel(**inputs):
    import concourse.bacc as bacc
    from concourse.bass_utils import run_bass_kernel_spmd

    nc = bacc.Bacc("TRN2", target_bir_lowering=False, num_devices=1)
    arrays, args = {}, []
    for name, a in layouts(inputs).items():
        a = np.ascontiguousarray(a)
        arrays[name + "_d"] = a
        args.append(nc.dram_tensor(name + "_d", a.shape, mybir.dt.from_np(a.dtype), kind="ExternalInput").ap())
    args.append(nc.dram_tensor("out_d", (P, KD, TOK), F32, kind="ExternalOutput").ap())
    program(nc, *args)
    r = run_bass_kernel_spmd(nc, [arrays], core_ids=[0])
    y = r.results[0]["out_d"]
    return np.ascontiguousarray(y.transpose(1, 0, 2).reshape(D, TOK).T)[None]
```
